# Optimizing a Trainium2 kernel written in Bass

```python
import jax, jax.numpy as jnp
from jax import lax
import numpy as np

D_MODEL = 1024
BATCH = 1
SEQ = 512
DEPTH = 1

CHUNK = 64
Q_BLOCK = 128
EPS = 1e-6
D_FF = 2816
N_MOD = 9
CONV_WIDTH = 512
CONV_GROUPS = 8
CONV_K = 3
MLA_HEADS = 4
QK_NOPE = 128
QK_ROPE = 64
V_HEAD = 128
Q_LORA = 384
KV_LORA = 256
ROPE_THETA = 10000.0
MLA_WIDTH = MLA_HEADS * V_HEAD
MIX_WIDTH = CONV_WIDTH + MLA_WIDTH
IN_COLS = 3 * CONV_WIDTH + Q_LORA + KV_LORA + QK_ROPE

kernel_name = "hymba_conv_mla_macaron_adaln_block"

def rmsnorm(x, g):
    xf = x.astype(jnp.float32)
    y = xf * lax.rsqrt(jnp.mean(xf * xf, axis=-1, keepdims=True) + EPS)
    return (y * g.astype(jnp.float32)).astype(x.dtype)

def group_rmsnorm(y, g, n_groups):
    b, s, w = y.shape
    yf = y.astype(jnp.float32).reshape(b, s, n_groups, w // n_groups)
    yf = yf * lax.rsqrt(jnp.mean(yf * yf, axis=-1, keepdims=True) + EPS)
    return (yf.reshape(b, s, w) * g.astype(jnp.float32)).astype(y.dtype)

def modulate(h, shift, scale):
    return h * (1.0 + scale[:, None, :]) + shift[:, None, :]

def swiglu(h, w1, w3, w2):
    return (jax.nn.silu(h @ w1) * (h @ w3)) @ w2

def rope(x, cos, sin):
    half = x.shape[-1] // 2
    x1, x2 = x[..., :half], x[..., half:]
    return jnp.concatenate([x1 * cos - x2 * sin, x1 * sin + x2 * cos], axis=-1)

def short_conv_mixer(xb, xc, xu, conv_w):
    u = xc * xu
    s = u.shape[1]
    up = jnp.pad(u, ((0, 0), (CONV_K - 1, 0), (0, 0)))
    y = conv_w[0] * up[:, 0:s]
    for k in range(1, CONV_K):
        y = y + conv_w[k] * up[:, k:k + s]
    return xb * y

def mla(cq, ckv, kr, positions, q_norm_g, w_uq, kv_norm_g, w_ukv):
    b, s, _ = cq.shape
    q = (rmsnorm(cq, q_norm_g) @ w_uq).reshape(b, s, MLA_HEADS, QK_NOPE + QK_ROPE)
    q_nope, q_rope = q[..., :QK_NOPE], q[..., QK_NOPE:]
    kv = (rmsnorm(ckv, kv_norm_g) @ w_ukv).reshape(b, s, MLA_HEADS, QK_NOPE + V_HEAD)
    k_nope, v = kv[..., :QK_NOPE], kv[..., QK_NOPE:]

    inv_freq = ROPE_THETA ** (-jnp.arange(0, QK_ROPE, 2, dtype=jnp.float32) / QK_ROPE)
    ang = positions.astype(jnp.float32)[..., None] * inv_freq
    cos = jnp.cos(ang).astype(cq.dtype)
    sin = jnp.sin(ang).astype(cq.dtype)
    q_rope = rope(q_rope, cos[:, :, None, :], sin[:, :, None, :])
    k_rope = rope(kr, cos, sin)

    scale = (QK_NOPE + QK_ROPE) ** -0.5
    nblk = s // Q_BLOCK
    qn_b = q_nope.reshape(b, nblk, Q_BLOCK, MLA_HEADS, QK_NOPE).transpose(1, 0, 2, 3, 4)
    qr_b = q_rope.reshape(b, nblk, Q_BLOCK, MLA_HEADS, QK_ROPE).transpose(1, 0, 2, 3, 4)
    k_chunk = jnp.arange(s) // CHUNK

    def block(args):
        i, qn, qr = args
        sc = (jnp.einsum('bqhd,bkhd->bhqk', qn, k_nope)
              + jnp.einsum('bqhd,bkd->bhqk', qr, k_rope)).astype(jnp.float32) * scale
        q_chunk = (i * Q_BLOCK + jnp.arange(Q_BLOCK)) // CHUNK
        mask = k_chunk[None, :] <= q_chunk[:, None]
        sc = jnp.where(mask[None, None], sc, jnp.float32(-1e30))
        p = jax.nn.softmax(sc, axis=-1).astype(v.dtype)
        return jnp.einsum('bhqk,bkhd->bqhd', p, v)

    o = lax.map(block, (jnp.arange(nblk), qn_b, qr_b))
    return o.transpose(1, 0, 2, 3, 4).reshape(b, s, MLA_WIDTH)

def setup_inputs(seed: int = 0) -> dict:
    key = jax.random.key(seed)
    ks = iter(jax.random.split(key, 32))
    f32 = jnp.float32
    L = DEPTH

    def nrm(shape, fan_in, scale=1.0):
        return jax.random.normal(next(ks), shape, f32) * (scale * fan_in ** -0.5)

    def gain(shape):
        return 1.0 + 0.05 * jax.random.normal(next(ks), shape, f32)

    x = jax.random.normal(next(ks), (BATCH, SEQ, D_MODEL), f32)
    c = jax.random.normal(next(ks), (BATCH, D_MODEL), f32)
    offset = jax.random.randint(next(ks), (BATCH, 1), 0, 4096)
    positions = (offset + jnp.arange(SEQ)[None, :]).astype(jnp.int32)
    return {
        "x": x,
        "c": c,
        "positions": positions,
        "ada_w": nrm((L, D_MODEL, N_MOD * D_MODEL), D_MODEL, 0.5),
        "ada_b": 0.02 * jax.random.normal(next(ks), (L, N_MOD * D_MODEL), f32),
        "norm_ffn1_g": gain((L, D_MODEL)),
        "ffn1_w1": nrm((L, D_MODEL, D_FF), D_MODEL),
        "ffn1_w3": nrm((L, D_MODEL, D_FF), D_MODEL),
        "ffn1_w2": nrm((L, D_FF, D_MODEL), D_FF),
        "norm_mix_g": gain((L, D_MODEL)),
        "w_in": nrm((L, D_MODEL, IN_COLS), D_MODEL),
        "conv_w": nrm((L, CONV_K, CONV_WIDTH), CONV_K),
        "q_norm_g": gain((L, Q_LORA)),
        "w_uq": nrm((L, Q_LORA, MLA_HEADS * (QK_NOPE + QK_ROPE)), Q_LORA),
        "kv_norm_g": gain((L, KV_LORA)),
        "w_ukv": nrm((L, KV_LORA, MLA_HEADS * (QK_NOPE + V_HEAD)), KV_LORA),
        "out_norm_g": gain((L, MIX_WIDTH)),
        "w_out": nrm((L, MIX_WIDTH, D_MODEL), MIX_WIDTH),
        "norm_ffn2_g": gain((L, D_MODEL)),
        "ffn2_w1": nrm((L, D_MODEL, D_FF), D_MODEL),
        "ffn2_w3": nrm((L, D_MODEL, D_FF), D_MODEL),
        "ffn2_w2": nrm((L, D_FF, D_MODEL), D_FF),
        "final_norm_g": gain((D_MODEL,)),
    }

def reference(x, c, positions, ada_w, ada_b, norm_ffn1_g, ffn1_w1, ffn1_w3, ffn1_w2,
              norm_mix_g, w_in, conv_w, q_norm_g, w_uq, kv_norm_g, w_ukv, out_norm_g,
              w_out, norm_ffn2_g, ffn2_w1, ffn2_w3, ffn2_w2, final_norm_g):
    b = x.shape[0]
    cuts = [CONV_WIDTH, 2 * CONV_WIDTH, 3 * CONV_WIDTH,
            3 * CONV_WIDTH + Q_LORA, 3 * CONV_WIDTH + Q_LORA + KV_LORA]
    for l in range(DEPTH):
        mod = (jax.nn.silu(c) @ ada_w[l] + ada_b[l]).reshape(b, N_MOD, D_MODEL)
        sh1, sc1, g1 = mod[:, 0], mod[:, 1], mod[:, 2]
        sh2, sc2, g2 = mod[:, 3], mod[:, 4], mod[:, 5]
        sh3, sc3, g3 = mod[:, 6], mod[:, 7], mod[:, 8]

        h = modulate(rmsnorm(x, norm_ffn1_g[l]), sh1, sc1)
        x = x + 0.5 * g1[:, None, :] * swiglu(h, ffn1_w1[l], ffn1_w3[l], ffn1_w2[l])

        h = modulate(rmsnorm(x, norm_mix_g[l]), sh2, sc2)
        z = h @ w_in[l]
        xb, xc, xu, cq, ckv, kr = jnp.split(z, cuts, axis=-1)
        y_a = short_conv_mixer(xb, xc, xu, conv_w[l])
        y_b = mla(cq, ckv, kr, positions, q_norm_g[l], w_uq[l], kv_norm_g[l], w_ukv[l])
        y_a = group_rmsnorm(y_a, out_norm_g[l, :CONV_WIDTH], CONV_GROUPS)
        y_b = group_rmsnorm(y_b, out_norm_g[l, CONV_WIDTH:], MLA_HEADS)
        y = jnp.concatenate([y_a, y_b], axis=-1) @ w_out[l]
        x = x + g2[:, None, :] * y

        h = modulate(rmsnorm(x, norm_ffn2_g[l]), sh3, sc3)
        x = x + 0.5 * g3[:, None, :] * swiglu(h, ffn2_w1[l], ffn2_w3[l], ffn2_w2[l])
    return rmsnorm(x, final_norm_g)


_drawn_inputs = setup_inputs


def setup_inputs(seed=0):
    import zlib

    import numpy as np

    out = dict(_drawn_inputs(seed))
    spreads = {}
    factors = {'norm_ffn1_g': 6.601,
     'norm_mix_g': 2.961,
     'q_norm_g': 8.0,
     'kv_norm_g': 5.431,
     'out_norm_g': 15.742,
     'norm_ffn2_g': 8.0}
    for name, (base, spread) in spreads.items():
        noise = np.random.default_rng([zlib.crc32(name.encode()), seed]).standard_normal(out[name].shape)
        drawn = base * np.exp(spread * noise) if base else spread * noise
        out[name] = __import__('jax').numpy.asarray(drawn.astype(out[name].dtype))
    for name, factor in factors.items():
        out[name] = (out[name] * factor).astype(out[name].dtype)
    return out
```

```python
from contextlib import ExitStack
import math

import concourse.bass as bass
from concourse import mybir

F32 = mybir.dt.float32
F32R = mybir.dt.float32r
I32 = mybir.dt.int32
ALU = mybir.AluOpType
ACT = mybir.ActivationFunctionType
AX_X = mybir.AxisListType.X

P = 128
D_MODEL, SEQ, D_FF, N_MOD = 1024, 512, 2816, 9
CONV_WIDTH, CONV_K, HEADS = 512, 3, 4
QK_NOPE, QK_ROPE, V_HEAD, Q_LORA, KV_LORA = 128, 64, 128, 384, 256
CHUNK, EPS, ROPE_THETA = 64, 1e-6, 10000.0
DT = D_MODEL // P
TT = SEQ // P
FT = D_FF // P
CT = CONV_WIDTH // P
QT, KT = Q_LORA // P, KV_LORA // P
UW = 1024
B_SPLIT = (8, 7, 7)
B_FROM = (0, 8, 15)
CQ0 = 3 * CONV_WIDTH
CKV0 = CQ0 + Q_LORA
KR0 = CKV0 + KV_LORA
QH = QK_NOPE + QK_ROPE
KVH = QK_NOPE + V_HEAD
SCALE = float(QH) ** -0.5

U_A1 = 0
U_B1 = U_A1 + 2 * FT
U_Z = U_B1 + 3 * DT
U_CONV = U_Z + QT + KT + 1
U_V = U_CONV + 3 * CT
U_H = U_V + KT
U_O = U_H + HEADS
U_A2 = U_O + DT
U_B2 = U_A2 + 2 * FT

N_FFN1, N_MIX, N_KV, N_Q, N_HEAD, N_FFN2, N_FINAL = 0, 1, 2, 3, 4, 8, 9
SQ_BASE = {N_FFN1: 0, N_MIX: 8, N_KV: 16, N_Q: 18, N_FFN2: 21, N_FINAL: 29}
SQ_TURN = {N_FFN1: 0, N_MIX: 1, N_KV: 2, N_Q: 3, N_FFN2: 4, N_FINAL: 5}
AP_BASE = {N_FFN1: 0, N_MIX: 8, N_KV: 16, N_Q: 18, N_HEAD: 25, N_FFN2: 29, N_FINAL: 37}
AP_CONV = 21
SPREAD = {N_FFN1: 0, N_MIX: 1, N_KV: 2, N_Q: 3, N_HEAD: 8, N_HEAD + 1: 9, N_HEAD + 2: 10, N_HEAD + 3: 11, N_FFN2: 12}
SPREAD_CONV = 4

K_IDENT, K_DUP, K_DUP32, K_HALF, K_ONE, K_ROPE = 0, 128, 256, 384, 416, 417
K_COLS = 420
K_ALL = K_COLS + 3 * P
SQUARE = 32
QUARTERS = P // SQUARE

V_ADAB, V_C, V_G1, V_GMIX, V_G2, V_GFIN = 0, 72, 80, 88, 96, 104
V_QG, V_KVG, V_OUTG, V_CONV = 112, 115, 117, 125
V_COLS, V_ROWS1 = 137, 112

TURN = 2.0 * math.pi
TURN1 = 6.28125
TURN2 = round((TURN - TURN1) * 2.0 ** 20) / 2.0 ** 20
TURN3 = TURN - TURN1 - TURN2
ROUND = 12582912.0
SIN_MAX = 3.1415925
LAG = 3
FREE = 1


def hybrid_block(nc, x, c, positions, ada_w, ada_b, norm_ffn1_g, ffn1_w1, ffn1_w3, ffn1_w2, norm_mix_g,
                 w_in, conv_w, q_norm_g, w_uq, kv_norm_g, w_ukv, out_norm_g, w_out, norm_ffn2_g,
                 ffn2_w1, ffn2_w3, ffn2_w2, final_norm_g, consts, out):
    with ExitStack() as ctx:
        def sem(name):
            return ctx.enter_context(nc.semaphore(name))

        top = [16512]

        def at(name, shape, dt=F32, offset=None):
            n = 4
            for s in shape[1:]:
                n *= s
            if offset is None:
                offset = top[0]
                top[0] += -(-n // 32) * 32
            return nc.alloc_sbuf_tensor_at(name, shape, dt, offset=offset)

        def place(base, *specs):
            made = []
            for name, shape, dt in specs:
                made.append(at(name, shape, dt, base))
                n = 4
                for s in shape[1:]:
                    n *= s
                base += n
            return made, base

        xres = at("xres", [P, DT, SEQ])
        hh_at = top[0]
        hh = at("hh", [P, DT, SEQ], F32R)
        hl_at = top[0]
        hl = at("hl", [P, DT, SEQ], F32R)
        raw = [at(f"raw{b}", [P, UW]) for b in range(2)]
        wh = [at(f"wh{b}", [P, UW], F32R) for b in range(2)]
        wl = [at(f"wl{b}", [P, UW], F32R) for b in range(2)]
        kst = at("kst", [P, K_COLS + 2])
        vcol = at("vcol", [P, V_COLS + 10])
        mods = at("mods", [P, N_MOD * DT])
        silu_c = at("silu_c", [P, DT])
        sig_c = at("sig_c", [P, DT])
        a_cols = at("a_cols", [P, 3, DT])
        half_gates = at("half_gates", [P, 2, DT])
        cs = at("cs", [P, SEQ])
        rms = at("rms", [P, TT])
        rrms = at("rrms", [P, TT])
        rrms_h = at("rrms_h", [P, TT], F32R)
        rrms_l = at("rrms_l", [P, TT])
        folded = at("folded", [P, D_MODEL // SQUARE])
        exact = at("exact", [P, 3, P], F32R)
        nmax_s = at("nmax_s", [P, HEADS * TT])
        nmax = at("nmax", [P, HEADS * TT])
        rsum = at("rsum", [P, HEADS * TT])
        rinv = at("rinv", [P, HEADS * TT])
        u_at = top[0]
        ubuf = at("ubuf", [P, 3, SEQ])
        (sigb, sbuf, gbuf), _ = place(u_at, ("sigb", [P, SEQ], F32), ("sbuf", [P, SEQ], F32), ("gbuf", [P, SEQ], F32))
        sq_at = top[0]
        sq = at("sq", [P, 2, SEQ])
        sacc = at("sacc", [P, SEQ])
        (group_rh, _, group_rl), _ = place(sq_at, ("group_rh", [P, SEQ], F32R), ("group_gap", [P, SEQ], F32),
                                           ("group_rl", [P, SEQ], F32R))
        diag_at = top[0]
        diag = at("diag", [P, 2, TT, P], F32R)
        (turned,), _ = place(diag_at, ("turned", [P, D_MODEL], F32))
        region = top[0]
        (gh, gl, ada_ring, acc), end = place(region, ("gh", [P, FT, SEQ], F32R), ("gl", [P, FT, SEQ], F32R),
                                             ("ada_ring", [P, 4, D_MODEL], F32), ("acc", [P, D_MODEL], F32))
        assert end <= 229344, end
        (ada_start, x_nat, vec1, vec2, kst2), e2 = place(region, ("ada_start", [P, 16, D_MODEL], F32),
                                                   ("x_nat", [P, TT, D_MODEL], F32), ("vec1", [P, P], F32),
                                                   ("vec2", [P, P], F32), ("kst2", [P, 3, P], F32))
        (pos, posf, ang, turns), e2 = place(e2, ("pos", [P, SEQ], I32), ("posf", [P, SEQ], F32),
                                            ("ang", [P, SEQ], F32), ("turns", [P, SEQ], F32))
        assert e2 <= end, e2
        (zkv, zq, ckh, ckl, cqh, cql), e3 = place(
            region, ("zkv", [P, KT, SEQ], F32), ("zq", [P, QT, SEQ], F32),
            ("ckh", [P, KT, SEQ], F32R), ("ckl", [P, KT, SEQ], F32R),
            ("cqh", [P, QT, SEQ], F32R), ("cql", [P, QT, SEQ], F32R))
        (o_raw,), _ = place(region, ("o_raw", [P, HEADS, SEQ], F32))
        (krh, krl, qnh, qnl, qrh, qrl, knh, knl, vh, vl), e3 = place(
            e3, ("krh", [P, SEQ], F32R), ("krl", [P, SEQ], F32R),
            ("qnh", [P, 2, SEQ], F32R), ("qnl", [P, 2, SEQ], F32R),
            ("qrh", [P, 2, SEQ], F32R), ("qrl", [P, 2, SEQ], F32R),
            ("knh", [P, 2, SEQ], F32R), ("knl", [P, 2, SEQ], F32R),
            ("vh", [P, TT, HEADS * V_HEAD], F32R), ("vl", [P, TT, HEADS * V_HEAD], F32R))
        (cbuf, ubufc, cacc), _ = place(e3, ("cbuf", [P, SEQ], F32), ("ubufc", [P, SEQ], F32), ("cacc", [P, SEQ], F32))
        (pth, ptl, yc, probs, gsq, rope), e3 = place(
            e3, ("pth", [P, TT, SEQ], F32R), ("ptl", [P, TT, SEQ], F32R), ("yc", [P, CT, SEQ], F32),
            ("probs", [P, 2, TT * (TT + 1) // 2 * P], F32), ("gsq", [P, SEQ], F32), ("rope", [P, SEQ], F32))
        assert e3 <= 229344, e3
        (xg,), _ = place(hh_at, ("xg", [P, DT, SEQ], F32))
        (o_nat,), _ = place(hl_at, ("o_nat", [P, TT, D_MODEL], F32))

        pb = [ctx.enter_context(nc.psum_tensor(f"pb{i}", [P, SEQ], F32)) for i in range(8)]
        norm_bank = pb[7]

        ident = kst[:, K_IDENT:K_IDENT + P]
        one_col = kst[:, K_ONE:K_ONE + 1]

        exact_landed, exact_ready = sem("exact_landed"), sem("exact_ready")
        consts_landed, vecs_landed, pos_landed, x_landed = sem("consts_landed"), sem("vecs_landed"), sem("pos_landed"), sem("x_landed")
        start_landed = [sem(f"start_landed{i}") for i in range(8)]
        ada_landed = [sem(f"ada_landed{i}") for i in range(4)]
        raw_landed = [sem("raw_landed0"), sem("raw_landed1")]
        kn_landed = [sem("kn_landed0"), sem("kn_landed1")]
        hi_ready, lo_ready, unit_done = sem("hi_ready"), sem("lo_ready"), sem("unit_done")
        vec_turned, vec_ready, sigc_ready, siluc_ready = sem("vec_turned"), sem("vec_ready"), sem("sigc_ready"), sem("siluc_ready")
        cs_step, cs_ready = sem("cs_step"), sem("cs_ready")
        x_turned, x_copied = sem("x_turned"), sem("x_copied")
        ada_turned, ada_folded, ada_summed = sem("ada_turned"), sem("ada_folded"), sem("ada_summed")
        ada_step, mods_ready, cols_ready = sem("ada_step"), sem("mods_ready"), sem("cols_ready")
        sq_ready, sq_added, sacc_clear = sem("sq_ready"), sem("sq_added"), sem("sacc_clear")
        col_done, rms_ready, rrms_ready, diag_ready, bc_done = sem("col_done"), sem("rms_ready"), sem("rrms_ready"), sem("diag_ready"), sem("bc_done")
        rrms_split = sem("rrms_split")
        csq_ready, group_summed, group_rms_ready, group_step, group_r_ready = (
            sem("csq_ready"), sem("group_summed"), sem("group_rms_ready"), sem("group_step"), sem("group_r_ready"))
        u_ready, hh_ready, hl_ready = sem("u_ready"), sem("hh_ready"), sem("hl_ready")
        sig_ready, s_ready, g_ready, gh_ready, gl_ready = sem("sig_ready"), sem("s_ready"), sem("g_ready"), sem("gh_ready"), sem("gl_ready")
        x_upd = sem("x_upd")
        zkv_copied, zq_copied = sem("zkv_copied"), sem("zq_copied")
        kr_roped, kr_dup, krh_ready, krl_ready = sem("kr_roped"), sem("kr_dup"), sem("krh_ready"), sem("krl_ready")
        c_copied, u_conv, conv_step, yc_ready = sem("c_copied"), sem("u_conv"), sem("conv_step"), sem("yc_ready")
        vh_ready, vl_ready = sem("vh_ready"), sem("vl_ready")
        q_done, ph_ready, pl_ready, q_roped = sem("q_done"), sem("ph_ready"), sem("pl_ready"), sem("q_roped")
        s_done, max_ready, nmax_ready = sem("s_done"), sem("max_ready"), sem("nmax_ready")
        exp_ready, rinv_ready, p_ready = sem("exp_ready"), sem("rinv_ready"), sem("p_ready")
        t_done, pth_ready, ptl_ready = sem("t_done"), sem("pth_ready"), sem("ptl_ready")
        pv_done, o_copied, gsq_ready = sem("pv_done"), sem("o_copied"), sem("gsq_ready")
        xg_ready, xg_turned, o_scaled, out_stored = sem("xg_ready"), sem("xg_turned"), sem("o_scaled"), sem("out_stored")
        o_moved = [sem("even_o_moved"), sem("odd_o_moved")]

        w1v = [w[0].rearrange("(k p) f -> p k f", p=P) for w in (ffn1_w1, ffn2_w1)]
        w3v = [w[0].rearrange("(k p) f -> p k f", p=P) for w in (ffn1_w3, ffn2_w3)]
        w2v = [w[0].rearrange("(k p) f -> p k f", p=P) for w in (ffn1_w2, ffn2_w2)]
        winv = w_in[0].rearrange("(k p) f -> p k f", p=P)
        woutv = w_out[0].rearrange("(k p) f -> p k f", p=P)
        wuqv = w_uq[0].rearrange("(k p) (h f) -> p k h f", p=P, h=HEADS)
        wukvv = w_ukv[0].rearrange("(k p) (h f) -> p k h f", p=P, h=HEADS)
        adav = ada_w[0].rearrange("(k p) f -> p k f", p=P)

        def z_tile(i):
            return CONV_WIDTH + i * P, 2 * CONV_WIDTH + i * P, i * P

        def cols(t, k, n=P):
            return t[:, k * n:(k + 1) * n]

        CONV_BANKS = ((0, 1, 2), (3, 4, 6))
        OUT_BANK = (0, 1, 4, 5)
        O_BANK = (0, 1, 2, 3, 4, 5, 0, 1)
        O_UNITS = ((0, 0), (0, 1), (0, 2), (1, 0), (1, 1), (1, 2), (0, 3), (1, 3))
        P_OFF = [P * i * (i + 1) // 2 for i in range(TT + 1)]

        TILE_OF = tuple(reversed(range(TT)))

        def turn_bank(h, q):
            return pb[5 + (5 * h + q) % 2]

        block = ctx.enter_context(nc.Block())

        @block.sync
        def _(sp):
            sp.dma_start(kst[:, 0:K_COLS], consts[:, 0:K_COLS]).then_inc(consts_landed, 16)
            sp.dma_start(pos[:, :], positions.partition_broadcast(P).rearrange("p a s -> p (a s)")).then_inc(pos_landed, 16)
            sp.dma_start(x_nat[:, :, :], x[0].rearrange("(t p) d -> p t d", p=P)).then_inc(x_landed, 16)
            row = 0
            for v, n in ((ada_b, 72), (c, 8), (norm_ffn1_g, 8), (norm_mix_g, 8), (norm_ffn2_g, 8)):
                sp.dma_start(vec1[row:row + n, :], v[0].rearrange("(r q) -> r q", q=P)).then_inc(vecs_landed, 16)
                row += n
            sp.dma_start(vec1[row:row + 8, :], final_norm_g.rearrange("(r q) -> r q", q=P)).then_inc(vecs_landed, 16)
            row = 0
            for v, n in ((q_norm_g, QT), (kv_norm_g, KT), (out_norm_g, DT)):
                sp.dma_start(vec2[row:row + n, :], v[0].rearrange("(r q) -> r q", q=P)).then_inc(vecs_landed, 16)
                row += n
            sp.dma_start(vec2[row:row + CONV_K * CT, :],
                         conv_w[0].rearrange("t (r q) -> (t r) q", q=P)).then_inc(vecs_landed, 16)
            sp.dma_start(kst2[:, :, :], consts[:, K_COLS:K_ALL].rearrange("p (a b) -> p a b", a=3)).then_inc(exact_landed, 16)

            def start_load(i):
                col = D_MODEL if i < 4 else 0
                k = 2 * (i % 4)
                sp.dma_start(ada_start[:, 2 * i:2 * i + 2, :], adav[:, k:k + 2, col:col + D_MODEL]).then_inc(start_landed[i], 16)

            def load(n, par, src, width=UW):
                if not isinstance(n, int) or n > 2:
                    sp.wait_ge(lo_ready, n - 1)
                shape = list(src.shape)[1:]
                dst = raw[par][:, 0:width]
                if len(shape) == 2:
                    dst = dst.rearrange("p (k f) -> p k f", k=shape[0])
                sp.dma_start(dst, src).then_inc(raw_landed[par], 16)

            def up_units(base, f, i):
                col = sp.snap(i * P)
                load(base + 2 * i, 0, w1v[f][:, :, bass.ds(col, P)])
                load(base + 2 * i + 1, 1, w3v[f][:, :, bass.ds(col, P)])

            def down_units(base, f):
                with sp.Fori(0, DT // 2) as m:
                    for s in range(6):
                        p, kk = divmod(s, 3)
                        k0, n = B_FROM[kk], B_SPLIT[kk]
                        col = sp.snap(m * (2 * P) + p * P)
                        load(base + 6 * m + s, s % 2, w2v[f][:, k0:k0 + n, bass.ds(col, P)], n * P)

            for i in range(4):
                start_load(i)
            sp.dma_start(raw[0].rearrange("p (k f) -> p k f", k=DT), w1v[0][:, :, 0:P]).then_inc(raw_landed[0], 16)
            sp.dma_start(raw[1].rearrange("p (k f) -> p k f", k=DT), w3v[0][:, :, 0:P]).then_inc(raw_landed[1], 16)
            for i in range(4, 8):
                start_load(i)
            with sp.Fori(1, FT) as i:
                up_units(U_A1, 0, i)
            down_units(U_B1, 0)
            for j, c0 in enumerate([CKV0 + P * t for t in range(KT)] + [CQ0 + P * t for t in range(QT)]):
                load(U_Z + j, j % 2, winv[:, :, c0:c0 + P])
            load(U_Z + KT + QT, 1, winv[:, :, KR0:KR0 + QK_ROPE], DT * QK_ROPE)
            with sp.Fori(1, CT // 2 + 1) as m:
                for s in range(6):
                    p, which = divmod(s, 3)
                    c0 = z_tile(p)[which] - 2 * P
                    load(U_CONV - 6 + 6 * m + s, s % 2, winv[:, :, bass.ds(m * (2 * P) + c0, P)])
            for k in range(KT):
                load(U_V + k, k % 2, wukvv[:, k, :, QK_NOPE:KVH], HEADS * V_HEAD)
            for h in range(HEADS):
                load(U_H + h, h % 2, wuqv[:, :, h, :], QT * QH)
                sp.dma_start(raw[h % 2][:, QT * QH:QT * QH + KT * QK_NOPE].rearrange("p (k f) -> p k f", k=KT),
                             wukvv[:, :, h, 0:QK_NOPE]).then_inc(kn_landed[h % 2], 16)
            for o, (upper, pair) in enumerate(O_UNITS):
                load(U_O + o, o % 2, woutv[:, 4 * upper:4 * upper + 4, 2 * P * pair:2 * P * (pair + 1)])
            with sp.Fori(0, FT) as i:
                up_units(U_A2, 1, i)
            down_units(U_B2, 1)
            outv = out[0].rearrange("(t p) d -> p t d", p=P)
            for t in range(TT):
                sp.wait_ge(o_scaled, t + 1)
                sp.dma_start(outv[:, t, :], o_nat[:, t, :]).then_inc(out_stored, 16)
            sp.wait_ge(out_stored, 16 * TT)

        @block.gpsimd
        def _(pool):
            pool.wait_ge(sacc_clear, 1)
            for k in range(DT):
                pool.wait_ge(sq_ready, k + 1)
                pool.wait_ge(sq_added, k)
                pool.tensor_tensor(sacc[:, :], sacc[:, :], sq[:, k % 2, :], ALU.add).then_inc(sq_added, 1)
            for n in range(2):
                pool.wait_ge(hi_ready, n + 1)
                pool.tensor_tensor(wl[n][:, :], raw[n][:, :], wh[n][:, :].bitcast(F32), ALU.subtract).then_inc(lo_ready, 1)
            pool.wait_ge(mods_ready, 2)
            with pool.Fori(0, N_MOD - 2) as j:
                for k in range(DT):
                    pool.wait_ge(ada_step, 2 * DT + j * DT + k - 3)
                    pool.dma_start(ada_ring[:, k % 4, :], adav[:, k, bass.ds(j * D_MODEL + 2 * D_MODEL, D_MODEL)]) \
                        .then_inc(ada_landed[k % 4], 16)

        @block.scalar
        def _(act):
            def split_hi(n, par, landed):
                act.wait_ge(raw_landed[par], landed)
                if not isinstance(n, int) or n >= 2:
                    act.wait_ge(unit_done, n - 1)
                act.activation(wh[par][:, :], raw[par][:, :], ACT.Copy).then_inc(hi_ready, 1)

            def landed(n):
                return 16 * (n // 2 + 1)

            def square(idx, slot, src):
                if not isinstance(idx, int) or idx >= 2:
                    act.wait_ge(sq_added, idx - 1)
                act.activation(sq[:, slot, :], src, ACT.Square).then_inc(sq_ready, 1)

            def root(n, width):
                act.wait_ge(col_done, n + 1)
                act.activation(rms[:, :], norm_bank[:, 0:TT], ACT.Sqrt, scale=1.0 / width,
                               bias=kst[:, K_COLS:K_COLS + 1]).then_inc(rms_ready, 1)

            def sqrt_table(spare):
                act.activation(vcol[:, V_COLS + spare:V_COLS + spare + 1], kst[:, K_COLS:K_COLS + 1], ACT.Sqrt)

            def norm_hi(idx, dst, shift=None):
                act.wait_ge(u_ready, idx + 1)
                if shift is None:
                    act.activation(dst, ubuf[:, idx % 3, :], ACT.Copy).then_inc(hh_ready, 1)
                else:
                    act.activation(dst, ubuf[:, idx % 3, :], ACT.Identity, bias=shift).then_inc(hh_ready, 1)

            def norm_model(n, shift_mod):
                for k in range(DT):
                    s = shift_mod * DT + k
                    norm_hi(AP_BASE[n] + k, hh[:, k, :], mods[:, s:s + 1])

            def up(base, f):
                with act.Fori(0, FT) as i:
                    act.wait_ge(unit_done, base + 2 * i + 1)
                    act.wait_ge(s_ready, FREE + f * FT + i)
                    act.activation(sigb[:, :], pb[0][:, :], ACT.Sigmoid).then_inc(sig_ready, 1)
                    split_hi(base + 2 * i + 2, 0, 16 * i + landed(base + 2))
                    split_hi(base + 2 * i + 3, 1, 16 * i + landed(base + 2))
                    act.wait_ge(g_ready, FREE + f * FT + i + 1)
                    act.activation(gh[:, bass.ds(i, 1), :], gbuf[:, :].unsqueeze(1), ACT.Copy).then_inc(gh_ready, 1)

            def down(base, n, upd, final=False):
                with act.Fori(0, DT // 2) as m:
                    for s in range(6):
                        p, kk = divmod(s, 3)
                        split_hi(base + 6 * m + s + 2, s % 2, 48 * m + landed(base + s + 2))
                        if kk == 2:
                            act.wait_ge(x_upd, upd + 2 * m + p + 1)
                            square(SQ_BASE[n] + 2 * m + p, (SQ_BASE[n] + p) % 2, xres[:, bass.ds(2 * m + p, 1), :])

            act.wait_ge(vec_ready, 3)
            act.activation(sig_c[:, :], vcol[:, V_C:V_C + DT], ACT.Sigmoid).then_inc(sigc_ready, 1)
            act.wait_ge(cs_step, 10)
            act.activation(cs[:, :], ang[:, :], ACT.Sin).then_inc(cs_ready, 1)
            for k in range(DT):
                act.wait_ge(x_turned, k + 1)
                act.activation(xres[:, k, :], pb[k % 4][:, :], ACT.Copy).then_inc(x_copied, 1)
                act.wait_ge(x_copied, k + 1)
                square(k, k % 2, xres[:, k, :])
            sqrt_table(6)
            root(N_FFN1, D_MODEL)
            act.wait_ge(exact_landed, 16)
            act.activation(exact[:, :, :], kst2[:, :, :], ACT.Copy).then_inc(exact_ready, 1)
            split_hi(0, 0, 16)
            split_hi(1, 1, 16)
            act.wait_ge(mods_ready, 2)
            norm_model(N_FFN1, 0)

            up(U_A1, 0)
            down(U_B1, N_MIX, 0)

            sqrt_table(7)
            root(N_MIX, D_MODEL)
            norm_model(N_MIX, 3)
            for j in range(KT + QT + 1):
                act.wait_ge(unit_done, U_Z + j + 1)
                if j < KT:
                    act.activation(zkv[:, j, :], pb[j][:, :], ACT.Copy).then_inc(zkv_copied, 1)
                    act.wait_ge(zkv_copied, j + 1)
                    square(SQ_BASE[N_KV] + j, (SQ_BASE[N_KV] + j) % 2, zkv[:, j, :])
                elif j < KT + QT:
                    q = j - KT
                    act.activation(zq[:, q, :], pb[j][:, :], ACT.Copy).then_inc(zq_copied, 1)
                    act.wait_ge(zq_copied, q + 1)
                    square(SQ_BASE[N_Q] + q, (SQ_BASE[N_Q] + q) % 2, zq[:, q, :])
                n = U_Z + j + 2
                if j + 2 == KT + QT:
                    act.wait_ge(raw_landed[1], landed(n))
                    act.wait_ge(unit_done, n - 1)
                    src = raw[1][:, 0:DT * QK_ROPE].rearrange("p (k f) -> p k f", k=DT)
                    dst = wh[1].rearrange("p (k f) -> p k f", k=DT)
                    act.activation(dst[:, :, 0:64], src, ACT.Copy)
                    act.activation(dst[:, :, 64:96], src[:, :, 32:64], ACT.Copy)
                    act.activation(dst[:, :, 96:128], src[:, :, 0:32], ACT.Copy).then_inc(hi_ready, 1)
                else:
                    split_hi(n, n % 2, landed(n))
                if j == KT:
                    root(N_KV, KV_LORA)
                if j == KT + 1:
                    for t in range(KT):
                        norm_hi(AP_BASE[N_KV] + t, ckh[:, t, :])
            root(N_Q, Q_LORA)
            with act.Fori(0, CT // 2) as m:
                for s in range(6):
                    p, which = divmod(s, 3)
                    if which == 0:
                        act.wait_ge(unit_done, U_CONV + 6 * m + s + 1)
                        act.wait_ge(u_conv, FREE + 2 * m + p)
                        act.activation(cbuf[:, :], pb[CONV_BANKS[p][0]][:, :], ACT.Copy).then_inc(c_copied, 1)
                    split_hi(U_CONV + 6 * m + s + 2, s % 2, 48 * m + landed(U_CONV + s + 2))
            def conv_square(j):
                act.wait_ge(yc_ready, FREE + j + 1)
                act.wait_ge(sq_added, SQ_BASE[N_Q] + QT)
                if j >= 2:
                    act.wait_ge(group_summed, j - 1)
                act.activation(sq[:, j % 2, :], yc[:, j, :], ACT.Square).then_inc(csq_ready, 1)

            conv_square(0)
            conv_square(1)
            for t in range(QT):
                norm_hi(AP_BASE[N_Q] + t, cqh[:, t, :])
            act.wait_ge(kr_dup, 1)
            act.activation(krh[:, :], pb[5][:, :], ACT.Copy).then_inc(krh_ready, 1)

            def head_square(h):
                if h >= 1:
                    act.wait_ge(col_done, N_HEAD + h)
                act.activation(gsq[:, :], o_raw[:, h, :], ACT.Square).then_inc(gsq_ready, 1)

            def head_hi(h):
                b = h % 2
                n = U_H + h
                act.wait_ge(raw_landed[b], landed(n))
                act.wait_ge(kn_landed[b], 16 * (h // 2 + 1))
                act.wait_ge(unit_done, n - 1)
                src = raw[b][:, 0:QT * QH].rearrange("p (k f) -> p k f", k=QT)
                nope = wh[b][:, 0:QT * P].rearrange("p (k f) -> p k f", k=QT)
                rp = wh[b][:, QT * P:2 * QT * P].rearrange("p (k f) -> p k f", k=QT)
                act.activation(nope, src[:, :, 0:QK_NOPE], ACT.Copy)
                act.activation(rp[:, :, 0:64], src[:, :, 128:192], ACT.Copy)
                act.activation(rp[:, :, 64:96], src[:, :, 160:192], ACT.Copy)
                act.activation(rp[:, :, 96:128], src[:, :, 128:160], ACT.Copy)
                act.activation(wh[b][:, 768:1024], raw[b][:, QT * QH:QT * QH + 256], ACT.Copy).then_inc(hi_ready, 1)

            def head_parts_hi(h):
                r = h % 2
                if h >= 2:
                    act.wait_ge(s_done, 4 * (h - 1))
                act.wait_ge(q_done, 2 * h + 1)
                act.activation(qnh[:, r, :], pb[0][:, :], ACT.Copy).then_inc(ph_ready, 1)
                act.wait_ge(q_roped, h + 1)
                act.activation(qrh[:, r, :], rope[:, :], ACT.Copy).then_inc(ph_ready, 1)
                act.wait_ge(unit_done, U_H + h + 1)
                act.activation(knh[:, r, :], pb[2][:, :], ACT.Copy).then_inc(ph_ready, 1)

            def exp(h, q):
                e, i = TT * h + q, TILE_OF[q]
                act.wait_ge(nmax_ready, e + 1)
                if h >= 2:
                    act.wait_ge(t_done, TT * (h - 2) + q + 1)
                act.activation(probs[:, h % 2, P_OFF[i]:P_OFF[i + 1]], pb[3 + q % 2][:, 0:P * (i + 1)], ACT.Exp,
                               scale=SCALE, bias=nmax_s[:, e:e + 1], accum_out=rsum[:, e:e + 1]).then_inc(exp_ready, 1)

            def turned_hi(h, q):
                i = TILE_OF[q]
                act.wait_ge(t_done, TT * h + q + 1)
                act.wait_ge(pv_done, h)
                act.activation(pth[:, 0:i + 1, P * i:P * (i + 1)],
                               turn_bank(h, q)[:, 0:P * (i + 1)].rearrange("p (k q) -> p k q", k=i + 1),
                               ACT.Copy).then_inc(pth_ready, 1)

            def exps_and_turned(h):
                for q in range(TT):
                    exp(h + 1, q)
                    turned_hi(h, q)

            def head_out(h):
                act.wait_ge(pv_done, h + 1)
                act.activation(o_raw[:, h, :], turn_bank(h, 4)[:, :], ACT.Copy).then_inc(o_copied, 1)
                act.wait_ge(o_copied, h + 1)

            def unit_hi(n):
                split_hi(n, n % 2, landed(n))

            def conv_hi(j):
                norm_hi(AP_CONV + j, hh[:, j, :])

            def head_norm_hi(h):
                norm_hi(AP_BASE[N_HEAD] + h, hh[:, CT + h, :])

            head_hi(0)
            for t in range(TT):
                act.wait_ge(unit_done, U_V + KT)
                act.activation(vh[:, t, :], pb[t][:, :], ACT.Copy).then_inc(vh_ready, 1)
            conv_square(2)
            conv_square(3)
            head_hi(1)
            act.wait_ge(group_summed, CT)
            act.activation(sq[:, 0, :], pb[6][:, :], ACT.Sqrt, scale=1.0 / (CONV_WIDTH // 8),
                           bias=kst[:, K_COLS:K_COLS + 1]).then_inc(group_rms_ready, 1)
            head_parts_hi(0)
            head_hi(2)
            head_parts_hi(1)
            conv_hi(0)
            head_hi(3)
            for q in range(TT):
                exp(0, q)
            head_parts_hi(2)
            unit_hi(U_O)
            conv_hi(1)
            exps_and_turned(0)
            head_parts_hi(3)
            unit_hi(U_O + 1)
            conv_hi(2)
            head_out(0)
            head_square(0)
            exps_and_turned(1)
            conv_hi(3)
            head_out(1)
            root(N_HEAD, V_HEAD)
            head_square(1)
            exps_and_turned(2)
            head_norm_hi(0)
            head_out(2)
            unit_hi(U_O + 2)
            root(N_HEAD + 1, V_HEAD)
            head_square(2)
            for q in range(TT):
                turned_hi(3, q)
            head_norm_hi(1)
            unit_hi(U_O + 3)
            root(N_HEAD + 2, V_HEAD)
            head_out(3)
            head_norm_hi(2)
            head_square(3)
            unit_hi(U_O + 4)
            root(N_HEAD + 3, V_HEAD)
            head_norm_hi(3)
            for o in range(3, len(O_UNITS)):
                upper, pair = O_UNITS[o]
                unit_hi(U_O + o + 2)
                if upper:
                    for d in (2 * pair, 2 * pair + 1):
                        act.wait_ge(x_upd, DT + d + 1)
                        square(SQ_BASE[N_FFN2] + d, (SQ_BASE[N_FFN2] + d) % 2, xres[:, d, :])
            sqrt_table(8)
            root(N_FFN2, D_MODEL)
            norm_model(N_FFN2, 6)

            up(U_A2, 1)
            with act.Fori(0, DT // 2 - 1) as m:
                for s in range(6):
                    p, kk = divmod(s, 3)
                    split_hi(U_B2 + 6 * m + s + 2, s % 2, 48 * m + landed(U_B2 + s + 2))
                    if kk == 2:
                        act.wait_ge(x_upd, 2 * DT + 2 * m + p + 1)
                        square(SQ_BASE[N_FINAL] + 2 * m + p, (SQ_BASE[N_FINAL] + p) % 2, xres[:, bass.ds(2 * m + p, 1), :])
                        act.activation(xg[:, bass.ds(2 * m + p, 1), :], xres[:, bass.ds(2 * m + p, 1), :], ACT.Copy,
                                       scale=vcol[:, bass.ds(2 * m + p + V_GFIN, 1)]).then_inc(xg_ready, 1)
            for s in range(6):
                p, kk = divmod(s, 3)
                d = DT - 2 + p
                if s < 4:
                    n = U_B2 + 3 * (DT - 2) + s + 2
                    split_hi(n, n % 2, landed(n))
                if kk == 2:
                    act.wait_ge(x_upd, 2 * DT + d + 1)
                    square(SQ_BASE[N_FINAL] + d, (SQ_BASE[N_FINAL] + d) % 2, xres[:, d, :])
                    act.activation(xg[:, d, :], xres[:, d, :], ACT.Copy, scale=vcol[:, V_GFIN + d:V_GFIN + d + 1]).then_inc(xg_ready, 1)
            sqrt_table(9)
            root(N_FINAL, D_MODEL)
            for k in range(1, DT, 2):
                act.wait_ge(xg_turned, k + 1)
                act.activation(o_nat[:, :, k * P:(k + 1) * P], pb[OUT_BANK[k % 4]][:, :].rearrange("p (t d) -> p t d", t=TT),
                               ACT.Copy).then_inc(o_moved[1], 1)

        @block.tensor
        def _(pe):
            def three(o, pairs, start, stop, check=False):
                last = None
                for j, (sh, sl, mh, ml) in enumerate(pairs):
                    for t, (a, b) in enumerate(((sh, mh), (sh, ml), (sl, mh))):
                        last = pe.matmul(o, a, b, start=start and j == 0 and t == 0,
                                         stop=stop and j == len(pairs) - 1 and t == 2)
                return last

            def unit(n):
                pe.wait_ge(lo_ready, n + 1)

            def h_product(o, b, hbase):
                for k in range(DT):
                    pe.wait_ge(hl_ready, hbase + k + 1)
                    last = three(o, [(cols(wh[b], k), cols(wl[b], k), hh[:, k, :], hl[:, k, :])], k == 0, k == DT - 1)
                return last

            def norm_sum(n, src, applied):
                if n >= 1:
                    pe.wait_ge(u_ready, applied)
                for t in range(TT):
                    last = pe.matmul(norm_bank[:, t:t + 1], src[:, t * P:(t + 1) * P], one_col, start=True, stop=True)
                last.then_inc(col_done, 1)

            def norm_spread(n):
                for part in range(2):
                    pe.wait_ge(diag_ready, 2 * n + part + 1)
                    last = pe.matmul(norm_bank[:, :], exact[:, 0, :], diag[:, part, :, :], start=part == 0, stop=part == 1)
                last.then_inc(bc_done, 1)

            def first_pair(base, hbase):
                unit(base)
                unit(base + 1)
                for k in range(DT + LAG):
                    for b, kb in ((0, k), (1, k - LAG)):
                        if not 0 <= kb < DT:
                            continue
                        pe.wait_ge(hl_ready, hbase + kb + 1)
                        last = three(pb[b][:, :], [(cols(wh[b], kb), cols(wl[b], kb), hh[:, kb, :], hl[:, kb, :])],
                                     kb == 0, kb == DT - 1)
                        if kb == DT - 1:
                            last.then_inc(unit_done, 1)

            def up_tile(base, f, i, n_norm):
                unit(base + 2 * i)
                pe.wait_ge(s_ready, FREE + f * FT + i)
                h_product(pb[0][:, :], 0, AP_BASE[n_norm]).then_inc(unit_done, 1)
                unit(base + 2 * i + 1)
                pe.wait_ge(g_ready, FREE + f * FT + i)
                h_product(pb[1][:, :], 1, AP_BASE[n_norm]).then_inc(unit_done, 1)

            def down(base, f, n_norm):
                with pe.Fori(0, DT // 2) as m:
                    for s in range(6):
                        p, kk = divmod(s, 3)
                        b = s % 2
                        unit(base + 6 * m + s)
                        if kk == 0:
                            pe.wait_ge(sq_added, SQ_BASE[n_norm] + 2 * m + p - 1)
                        for j in range(B_SPLIT[kk]):
                            k = B_FROM[kk] + j
                            pe.wait_ge(gl_ready, FREE + f * FT + k + 1)
                            last = three(pb[2 + p][:, :], [(cols(wh[b], j), cols(wl[b], j), gh[:, k, :], gl[:, k, :])],
                                         k == 0, k == FT - 1)
                        last.then_inc(unit_done, 1)

            pe.wait_ge(consts_landed, 16)
            pe.wait_ge(vecs_landed, 16 * 10)
            pe.transpose(pb[4][:, 0:V_ROWS1], vec1[0:V_ROWS1, :], ident[0:V_ROWS1, 0:V_ROWS1]).then_inc(vec_turned, 1)
            pe.transpose(pb[5][:, 0:V_COLS - V_ROWS1], vec2[0:V_COLS - V_ROWS1, :],
                         ident[0:V_COLS - V_ROWS1, 0:V_COLS - V_ROWS1]).then_inc(vec_turned, 1)
            pe.wait_ge(x_landed, 16)
            for k in range(DT):
                if k >= 4:
                    pe.wait_ge(x_copied, k - 3)
                for t in range(TT):
                    last = pe.transpose(pb[k % 4][:, t * P:(t + 1) * P], x_nat[:, t, k * P:(k + 1) * P], ident)
                last.then_inc(x_turned, 1)
            pe.wait_ge(sq_added, DT)
            norm_sum(N_FFN1, sacc, 0)
            pe.wait_ge(exact_ready, 1)
            norm_spread(N_FFN1)

            def mod_columns(v):
                pe.wait_ge(ada_folded, v + 1)
                pe.wait_ge(mods_ready, v)
                pe.matmul(pb[4][:, 0:D_MODEL // SQUARE], kst[:, K_DUP32:K_DUP32 + P], folded[:, :],
                          start=True, stop=True).then_inc(ada_summed, 1)

            pe.wait_ge(vec_ready, 1)
            mod_columns(0)
            mod_columns(1)

            first_pair(U_A1, AP_BASE[N_FFN1])
            with pe.Fori(0, (FT - 1) // 3) as j:
                for t in range(3):
                    up_tile(U_A1, 0, 3 * j + t + 1, N_FFN1)
                mod_columns(j + 2)
            down(U_B1, 0, N_MIX)
            pe.wait_ge(sq_added, SQ_BASE[N_MIX] + DT)
            norm_sum(N_MIX, sacc, AP_BASE[N_MIX])
            norm_spread(N_MIX)

            first_pair(U_Z, AP_BASE[N_MIX])
            for j in range(2, KT + QT + 1):
                unit(U_Z + j)
                h_product(pb[j][:, :], j % 2, AP_BASE[N_MIX]).then_inc(unit_done, 1)
                if j == KT:
                    pe.wait_ge(sq_added, SQ_BASE[N_KV] + KT)
                    norm_sum(N_KV, sacc, AP_BASE[N_KV])
                if j == KT + 1:
                    norm_spread(N_KV)
            pe.wait_ge(sq_added, SQ_BASE[N_Q] + QT)
            norm_sum(N_Q, sacc, AP_BASE[N_Q])
            with pe.Fori(0, CT // 2) as m:
                for s in range(6):
                    p, which = divmod(s, 3)
                    unit(U_CONV + 6 * m + s)
                    if which == 0:
                        pe.wait_ge(yc_ready, FREE + 2 * m)
                    h_product(pb[CONV_BANKS[p][which]][:, :], s % 2, AP_BASE[N_MIX]).then_inc(unit_done, 1)
            norm_spread(N_Q)
            pe.wait_ge(kr_roped, 1)
            pe.matmul(pb[5][:, :], kst[:, K_DUP:K_DUP + P], rope[:, :], start=True, stop=True).then_inc(kr_dup, 1)

            def v_unit(k):
                unit(U_V + k)
                if k == 0:
                    pe.wait_ge(yc_ready, FREE + CT)
                for t in range(TT):
                    last = three(pb[t][:, :], [(ckh[:, k, t * P:(t + 1) * P], ckl[:, k, t * P:(t + 1) * P],
                                                wh[k % 2][:, 0:HEADS * V_HEAD], wl[k % 2][:, 0:HEADS * V_HEAD])],
                                 k == 0, k == KT - 1)
                last.then_inc(unit_done, 1)

            def head_part(h, part):
                b = h % 2
                if part == 0:
                    unit(U_H + h)
                    pe.wait_ge(vl_ready, TT)
                    pe.wait_ge(pl_ready, 3 * h)
                    pe.wait_ge(hl_ready, AP_BASE[N_Q] + QT)
                if part < 2:
                    three(pb[part][:, :], [(cols(wh[b], QT * part + k), cols(wl[b], QT * part + k), cqh[:, k, :], cql[:, k, :])
                                           for k in range(QT)], True, True).then_inc(q_done, 1)
                else:
                    three(pb[2][:, :], [(cols(wh[b], 2 * QT + k), cols(wl[b], 2 * QT + k), ckh[:, k, :], ckl[:, k, :])
                                        for k in range(KT)], True, True).then_inc(unit_done, 1)

            def head_unit(h):
                for part in range(3):
                    head_part(h, part)

            def conv_sum(j):
                pe.wait_ge(csq_ready, j + 1)
                pe.matmul(pb[6][SQUARE * j:SQUARE * (j + 1), :], kst[:, K_HALF:K_HALF + SQUARE], sq[:, j % 2, :],
                          start=True, stop=True).then_inc(group_summed, 1)

            def conv_spread(j):
                rows = slice(SQUARE * j, SQUARE * (j + 1))
                pe.wait_ge(group_r_ready, 1)
                pe.wait_ge(u_ready, AP_CONV + j)
                pe.matmul(norm_bank[:, :], exact[rows, 1, :], group_rh[rows, :], start=True, stop=False)
                pe.matmul(norm_bank[:, :], exact[rows, 1, :], group_rl[rows, :], start=False, stop=True).then_inc(bc_done, 1)

            def scores(h, q):
                r, e, i = h % 2, TT * h + q, TILE_OF[q]
                if q == 0:
                    pe.wait_ge(pl_ready, 3 * h + 3)
                    pe.wait_ge(krl_ready, 1)
                if e >= 2:
                    pe.wait_ge(exp_ready, e - 1)
                n = P * (i + 1)
                qs = slice(P * i, n)
                bank = pb[3 + q % 2]
                three(bank[:, 0:n], [(qnh[:, r, qs], qnl[:, r, qs], knh[:, r, 0:n], knl[:, r, 0:n]),
                                     (qrh[:, r, qs], qrl[:, r, qs], krh[:, 0:n], krl[:, 0:n])], True, False)
                pe.matmul(bank[:, P * i:n], exact[0:SQUARE, 1, :], exact[0:SQUARE, 2, :],
                          start=False, stop=True).then_inc(s_done, 1)

            def bank_left(h, q):
                before = 5 * h + q - 2
                if before >= 0:
                    bh, bq = divmod(before, 5)
                    if bq == TT:
                        pe.wait_ge(o_copied, bh + 1)
                    else:
                        pe.wait_ge(ptl_ready, TT * bh + bq + 1)

            def turn(h, q):
                i = TILE_OF[q]
                bank_left(h, q)
                pe.wait_ge(p_ready, TT * h + q + 1)
                for kb in range(i + 1):
                    at_ = P_OFF[i] + P * kb
                    last = pe.transpose(turn_bank(h, q)[:, P * kb:P * (kb + 1)], probs[:, h % 2, at_:at_ + P], ident)
                last.then_inc(t_done, 1)

            def head_product(h):
                bank_left(h, TT)
                pe.wait_ge(ptl_ready, TT * h + TT)
                vs = slice(V_HEAD * h, V_HEAD * (h + 1))
                for kb in range(TT):
                    last = three(turn_bank(h, TT)[:, P * kb:SEQ], [(vh[:, kb, vs], vl[:, kb, vs], pth[:, kb, P * kb:SEQ],
                                                                   ptl[:, kb, P * kb:SEQ])], kb == 0, kb == TT - 1)
                last.then_inc(pv_done, 1)

            def scores_and_turns(h):
                for q in range(TT):
                    scores(h + 1, q)
                    turn(h, q)

            def head_sum(h):
                pe.wait_ge(gsq_ready, h + 1)
                norm_sum(N_HEAD + h, gsq, AP_BASE[N_HEAD] + h)

            def out_unit(o):
                upper, pair = O_UNITS[o]
                b = o % 2
                unit(U_O + o)
                if o == 0:
                    pe.wait_ge(pl_ready, 3 * HEADS)
                if o == 1:
                    pe.wait_ge(exp_ready, HEADS * TT)
                if o == 2:
                    pe.wait_ge(ptl_ready, HEADS * TT)
                    pe.wait_ge(o_copied, HEADS)
                if o == 6:
                    pe.wait_ge(x_upd, DT + 2)
                for k in range(4):
                    y = 4 * upper + k
                    pe.wait_ge(hl_ready, AP_CONV + y + 1)
                    for d in range(2):
                        w = slice((2 * k + d) * P, (2 * k + d + 1) * P)
                        last = three(pb[O_BANK[2 * pair + d]][:, :], [(wh[b][:, w], wl[b][:, w], hh[:, y, :], hl[:, y, :])],
                                     y == 0, y == DT - 1)
                last.then_inc(unit_done, 1)

            v_unit(0)
            v_unit(1)
            for j in range(CT):
                conv_sum(j)
            head_unit(0)
            head_unit(1)
            conv_spread(0)
            scores(0, 0)
            for q in range(1, TT):
                scores(0, q)
                head_part(2, q - 1)
            conv_spread(1)
            scores_and_turns(0)
            head_unit(3)
            conv_spread(2)
            head_product(0)
            scores_and_turns(1)
            conv_spread(3)
            head_product(1)
            head_sum(0)
            scores_and_turns(2)
            norm_spread(N_HEAD)
            head_product(2)
            out_unit(0)
            head_sum(1)
            for q in range(TT):
                turn(3, q)
            norm_spread(N_HEAD + 1)
            out_unit(1)
            head_sum(2)
            head_product(3)
            norm_spread(N_HEAD + 2)
            out_unit(2)
            head_sum(3)
            norm_spread(N_HEAD + 3)
            for o in range(3, len(O_UNITS)):
                out_unit(o)
            pe.wait_ge(sq_added, SQ_BASE[N_FFN2] + DT)
            norm_sum(N_FFN2, sacc, AP_BASE[N_FFN2])
            norm_spread(N_FFN2)

            pe.wait_ge(x_upd, 2 * DT)
            first_pair(U_A2, AP_BASE[N_FFN2])
            with pe.Fori(1, FT) as i:
                up_tile(U_A2, 1, i, N_FFN2)
            down(U_B2, 1, N_FINAL)
            for k in range(DT):
                pe.wait_ge(xg_ready, k + 1)
                if k >= 4:
                    pe.wait_ge(o_moved[k % 2], (k - 4) // 2 + 1)
                for t in range(TT):
                    last = pe.transpose(pb[OUT_BANK[k % 4]][:, t * P:(t + 1) * P], xg[:, k, t * P:(t + 1) * P], ident)
                last.then_inc(xg_turned, 1)
                if k == 3:
                    pe.wait_ge(sq_added, SQ_BASE[N_FINAL] + DT)
                    norm_sum(N_FINAL, sacc, AP_BASE[N_FINAL])

        @block.vector
        def _(dve):
            def split_lo(n, par):
                dve.wait_ge(hi_ready, n + 1)
                dve.tensor_tensor(wl[par][:, :], raw[par][:, :], wh[par][:, :].bitcast(F32), ALU.subtract).then_inc(lo_ready, 1)

            def clear_sum(n, previous):
                dve.wait_ge(col_done, previous + 1)
                dve.memset(sacc[:, :], 0.0).then_inc(sacc_clear, 1)

            def add_square(n, idx, slot):
                dve.wait_ge(sq_ready, idx + 1)
                dve.wait_ge(sacc_clear, SQ_TURN[n] + 1)
                dve.wait_ge(sq_added, idx)
                dve.tensor_tensor(sacc[:, :], sacc[:, :], sq[:, slot, :], ALU.add).then_inc(sq_added, 1)

            def inverse(n, spread=True):
                dve.wait_ge(rms_ready, n + 1)
                dve.reciprocal(rrms[:, :], rms[:, :]).then_inc(rrms_ready, 1)
                dve.wait_ge(rrms_ready, n + 1)
                if not spread:
                    return
                dve.tensor_copy(rrms_h[:, :], rrms[:, :]).then_inc(rrms_split, 1)
                dve.wait_ge(rrms_split, 2 * n + 1)
                dve.tensor_tensor(rrms_l[:, :], rrms[:, :], rrms_h[:, :].bitcast(F32), ALU.subtract).then_inc(rrms_split, 1)
                if n >= 1:
                    dve.wait_ge(bc_done, SPREAD[n])
                idb = ident.unsqueeze(1).to_broadcast([P, TT, P])
                for part, r in enumerate((rrms_h[:, :].bitcast(F32), rrms_l[:, :])):
                    dve.wait_ge(rrms_split, 2 * n + part + 1)
                    dve.tensor_tensor(diag[:, part, :, :], idb, r.unsqueeze(2).to_broadcast([P, TT, P]),
                                      ALU.mult).then_inc(diag_ready, 1)

            def apply(n, base, tiles, middle=None):
                def lo(j):
                    src, gain, shift, hi_t, lo_t = tiles[j]
                    idx = base + j
                    dve.wait_ge(hh_ready, idx + 1)
                    u = ubuf[:, idx % 3, :]
                    if shift is None:
                        dve.tensor_tensor(lo_t, u, hi_t.bitcast(F32), ALU.subtract).then_inc(hl_ready, 1)
                    else:
                        dve.scalar_tensor_tensor(out=lo_t, in0=u, scalar=shift, in1=hi_t.bitcast(F32),
                                                 op0=ALU.add, op1=ALU.subtract).then_inc(hl_ready, 1)
                dve.wait_ge(bc_done, n + 1)
                for j, (src, gain, shift, hi_t, lo_t) in enumerate(tiles):
                    idx = base + j
                    if idx >= 3:
                        dve.wait_ge(hl_ready, idx - 2)
                    dve.scalar_tensor_tensor(out=ubuf[:, idx % 3, :], in0=src, scalar=gain, in1=norm_bank[:, :],
                                             op0=ALU.mult, op1=ALU.mult).then_inc(u_ready, 1)
                    if middle is None:
                        if j >= 1:
                            lo(j - 1)
                        continue
                    if j == 2:
                        middle()
                    if j >= 2:
                        lo(j - 2)
                if middle is not None:
                    lo(len(tiles) - 2)
                lo(len(tiles) - 1)

            def apply_model(n, which, shift_mod, middle=None):
                apply(SPREAD[n], AP_BASE[n], [(xres[:, k, :], a_cols[:, which, k:k + 1],
                                       mods[:, shift_mod * DT + k:shift_mod * DT + k + 1], hh[:, k, :], hl[:, k, :])
                                      for k in range(DT)], middle)

            def ada(v, k, src, landed_sem, landed_value):
                dve.wait_ge(landed_sem, landed_value)
                dve.wait_ge(ada_step, DT * v + k)
                if k == 0:
                    dve.wait_ge(ada_turned, v)
                    dve.tensor_scalar(acc[:, :], src, silu_c[:, 0:1], None, ALU.mult).then_inc(ada_step, 1)
                else:
                    dve.scalar_tensor_tensor(out=acc[:, :], in0=src, scalar=silu_c[:, k:k + 1], in1=acc[:, :],
                                             op0=ALU.mult, op1=ALU.add).then_inc(ada_step, 1)

            def fold(v):
                dve.wait_ge(ada_step, DT * v + DT)
                dve.wait_ge(ada_folded, v)
                dve.wait_ge(bc_done, 1)
                dve.transpose(turned[:, :], acc[:, :]).then_inc(ada_turned, 1)
                dve.wait_ge(ada_turned, v + 1)
                dve.wait_ge(ada_summed, v)
                dve.tensor_reduce(folded[:, :], turned.rearrange("p (b c) -> p b c", c=SQUARE), AX_X,
                                  ALU.add).then_inc(ada_folded, 1)

            def mod_bias(v, col):
                dve.wait_ge(ada_summed, v + 1)
                for g in range(QUARTERS):
                    rows = slice(SQUARE * g, SQUARE * (g + 1))
                    sums = pb[4][rows, 0:D_MODEL // SQUARE].rearrange("p (k g) -> p k g", g=QUARTERS)[:, :, g]
                    last = dve.tensor_tensor(mods[rows, bass.ds(col, DT)], sums, vcol[rows, bass.ds(col, DT)], ALU.add)
                last.then_inc(mods_ready, 1)

            def up_tile(base, f, i, middle=None):
                dve.wait_ge(sig_ready, f * FT + i + 1)
                dve.wait_ge(g_ready, FREE + f * FT + i)
                dve.tensor_tensor(sbuf[:, :], sigb[:, :], pb[0][:, :], ALU.mult).then_inc(s_ready, 1)
                split_lo(base + 2 * i + 2, 0)
                if middle is not None:
                    middle()
                dve.wait_ge(unit_done, base + 2 * i + 2)
                dve.wait_ge(s_ready, FREE + f * FT + i + 1)
                dve.wait_ge(gl_ready, FREE + f * FT + i)
                dve.tensor_tensor(gbuf[:, :], sbuf[:, :], pb[1][:, :], ALU.mult).then_inc(g_ready, 1)
                split_lo(base + 2 * i + 3, 1)
                dve.wait_ge(gh_ready, f * FT + i + 1)
                dve.tensor_tensor(gl[:, bass.ds(i, 1), :], gbuf[:, :].unsqueeze(1), gh[:, bass.ds(i, 1), :].bitcast(F32),
                                  ALU.subtract).then_inc(gl_ready, 1)

            def update(d, bank, gate, done, upd):
                dve.wait_ge(unit_done, done)
                xd = xres[:, bass.ds(d, 1), :]
                dve.scalar_tensor_tensor(out=xd, in0=pb[bank][:, :].unsqueeze(1), scalar=gate, in1=xd,
                                         op0=ALU.mult, op1=ALU.add).then_inc(x_upd, 1)

            def down_pair(base, f, n, upd, m, splits=6):
                for s in range(6):
                    p, kk = divmod(s, 3)
                    if kk == 2:
                        d = 2 * m + p
                        update(d, 2 + p, half_gates[:, f, bass.ds(d, 1)], base + 6 * m + s + 1, upd)
                    if s < splits:
                        split_lo(base + 6 * m + s + 2, s % 2)
                    if kk == 2:
                        add_square(n, SQ_BASE[n] + 2 * m + p, (SQ_BASE[n] + p) % 2)

            dve.memset(kst[:, K_COLS:K_COLS + 1], EPS).then_inc(vec_ready, 1)
            dve.memset(sacc[:, :], 0.0).then_inc(sacc_clear, 1)
            for j, free in enumerate((s_ready, g_ready, gl_ready, u_conv, conv_step, yc_ready)):
                dve.memset(vcol[:, V_COLS + j:V_COLS + j + 1], 0.0).then_inc(free, 1)
            step = [0]

            def cs_next(ins):
                step[0] += 1
                ins.then_inc(cs_step, 1)
                dve.wait_ge(cs_step, step[0])

            freq, offset, phase = (kst[:, K_ROPE + i:K_ROPE + i + 1] for i in range(3))
            dve.wait_ge(pos_landed, 16)
            cs_next(dve.tensor_copy(posf[:, :], pos[:, :]))
            cs_next(dve.tensor_scalar(ang[:, :], posf[:, :], freq, None, ALU.mult))
            cs_next(dve.tensor_scalar(turns[:, :], ang[:, :], 1.0 / TURN, offset, ALU.mult, ALU.add))
            cs_next(dve.tensor_scalar(turns[:, :], turns[:, :], ROUND, None, ALU.add))
            cs_next(dve.tensor_scalar(turns[:, :], turns[:, :], ROUND, None, ALU.subtract))
            for part in (TURN1, TURN2):
                cs_next(dve.scalar_tensor_tensor(out=ang[:, :], in0=turns[:, :], scalar=-part, in1=ang[:, :],
                                                 op0=ALU.mult, op1=ALU.add))
            cs_next(dve.scalar_tensor_tensor(out=ang[:, :], in0=turns[:, :], scalar=-TURN3, in1=ang[:, :],
                                             op0=ALU.mult, op1=ALU.add))
            cs_next(dve.tensor_scalar(posf[:, :], ang[:, :], phase, SIN_MAX, ALU.add, ALU.min))
            dve.tensor_scalar(ang[:, :], posf[:, :], -SIN_MAX, None, ALU.max).then_inc(cs_step, 1)
            dve.wait_ge(vec_turned, 2)
            dve.tensor_copy(vcol[:, 0:V_ROWS1], pb[4][:, 0:V_ROWS1]).then_inc(vec_ready, 1)
            dve.tensor_copy(vcol[:, V_ROWS1:V_COLS], pb[5][:, 0:V_COLS - V_ROWS1]).then_inc(vec_ready, 1)
            dve.wait_ge(vec_ready, 3)
            dve.wait_ge(sigc_ready, 1)
            dve.tensor_tensor(silu_c[:, :], sig_c[:, :], vcol[:, V_C:V_C + DT], ALU.mult).then_inc(siluc_ready, 1)
            dve.wait_ge(siluc_ready, 1)
            for k in range(DT):
                ada(0, k, ada_start[:, k, :], start_landed[k // 2], 16)
            inverse(N_FFN1)
            fold(0)
            mod_bias(0, DT)
            dve.wait_ge(mods_ready, 1)
            dve.scalar_tensor_tensor(out=a_cols[:, 0, :], in0=mods[:, DT:2 * DT], scalar=1.0, in1=vcol[:, V_G1:V_G1 + DT],
                                     op0=ALU.add, op1=ALU.mult).then_inc(cols_ready, 1)
            dve.wait_ge(cols_ready, 1)

            def shift_vector():
                for k in range(DT):
                    ada(1, k, ada_start[:, DT + k, :], start_landed[4 + k // 2], 16)
                fold(1)
                mod_bias(1, 0)
                dve.wait_ge(mods_ready, 2)

            apply_model(N_FFN1, 0, 0, shift_vector)

            up_tile(U_A1, 0, 0)
            with dve.Fori(0, (FT - 1) // 3) as j:
                for t in range(3):
                    def some_ada(t=t):
                        for k in range(4 * t, min(4 * t + 4, DT)):
                            ada(j + 2, k, ada_ring[:, k % 4, :], ada_landed[k % 4], 32 * j + 16 * (k // 4 + 1))
                    up_tile(U_A1, 0, 3 * j + t + 1, some_ada)
                    if t == 1:
                        fold(j + 2)
                mod_bias(j + 2, j * DT + 2 * DT)
            dve.wait_ge(mods_ready, N_MOD)
            for which, mod, gain in ((1, 4, V_GMIX), (2, 7, V_G2)):
                dve.scalar_tensor_tensor(out=a_cols[:, which, :], in0=mods[:, mod * DT:(mod + 1) * DT], scalar=1.0,
                                         in1=vcol[:, gain:gain + DT], op0=ALU.add, op1=ALU.mult).then_inc(cols_ready, 1)
            for f, mod in ((0, 2), (1, 8)):
                dve.tensor_scalar(half_gates[:, f, :], mods[:, mod * DT:(mod + 1) * DT], 0.5, None, ALU.mult).then_inc(cols_ready, 1)
            dve.wait_ge(cols_ready, 5)
            clear_sum(N_MIX, N_FFN1)
            with dve.Fori(0, DT // 2) as m:
                down_pair(U_B1, 0, N_MIX, 0, m)
            inverse(N_MIX)
            apply_model(N_MIX, 1, 3)

            for j in range(KT + QT + 1):
                n = U_Z + j + 2
                if j == 0:
                    clear_sum(N_KV, N_MIX)
                if j == KT + 1:
                    apply(SPREAD[N_KV], AP_BASE[N_KV], [(zkv[:, t, :], vcol[:, V_KVG + t:V_KVG + t + 1], None, ckh[:, t, :], ckl[:, t, :])
                                                for t in range(KT)])
                if j + 2 == KT + QT:
                    dve.wait_ge(hi_ready, n + 1)
                    src = raw[1][:, 0:DT * QK_ROPE].rearrange("p (k f) -> p k f", k=DT)
                    hi = wh[1].rearrange("p (k f) -> p k f", k=DT).bitcast(F32)
                    lo = wl[1].rearrange("p (k f) -> p k f", k=DT)
                    dve.tensor_tensor(lo[:, :, 0:64], src, hi[:, :, 0:64], ALU.subtract)
                    dve.tensor_tensor(lo[:, :, 64:96], src[:, :, 32:64], hi[:, :, 64:96], ALU.subtract)
                    dve.tensor_tensor(lo[:, :, 96:128], src[:, :, 0:32], hi[:, :, 96:128], ALU.subtract).then_inc(lo_ready, 1)
                else:
                    split_lo(n, n % 2)
                if j < KT:
                    add_square(N_KV, SQ_BASE[N_KV] + j, (SQ_BASE[N_KV] + j) % 2)
                elif j < KT + QT:
                    q = j - KT
                    if q == 0:
                        inverse(N_KV)
                        clear_sum(N_Q, N_KV)
                    add_square(N_Q, SQ_BASE[N_Q] + q, (SQ_BASE[N_Q] + q) % 2)
            dve.wait_ge(unit_done, U_CONV)
            dve.wait_ge(cs_ready, 1)
            dve.tensor_tensor(rope[:, :], pb[5][:, :], cs[:, :], ALU.mult).then_inc(kr_roped, 1)
            inverse(N_Q)

            with dve.Fori(0, CT // 2) as m:
                for s in range(6):
                    p, which = divmod(s, 3)
                    i = 2 * m + p
                    banks = CONV_BANKS[p]
                    if which == 1:
                        dve.wait_ge(c_copied, i + 1)
                        dve.wait_ge(unit_done, U_CONV + 6 * m + s + 1)
                        dve.wait_ge(conv_step, FREE + 3 * i)
                        dve.tensor_tensor(ubufc[:, :], cbuf[:, :], pb[banks[1]][:, :], ALU.mult).then_inc(u_conv, 1)
                    if which == 2:
                        def tap(k):
                            return vcol[:, bass.ds(i + (V_CONV + CT * k), 1)]
                        dve.wait_ge(u_conv, FREE + i + 1)
                        dve.wait_ge(yc_ready, FREE + i)
                        dve.tensor_scalar(cacc[:, :], ubufc[:, :], tap(2), None, ALU.mult).then_inc(conv_step, 1)
                        for back in (1, 2):
                            dve.wait_ge(conv_step, FREE + 3 * i + back)
                            dve.scalar_tensor_tensor(out=cacc[:, back:SEQ], in0=ubufc[:, 0:SEQ - back], scalar=tap(2 - back),
                                                     in1=cacc[:, back:SEQ], op0=ALU.mult, op1=ALU.add).then_inc(conv_step, 1)
                        dve.wait_ge(conv_step, FREE + 3 * i + 3)
                        dve.wait_ge(unit_done, U_CONV + 6 * m + s + 1)
                        dve.tensor_tensor(yc[:, bass.ds(i, 1), :], cacc[:, :].unsqueeze(1), pb[banks[2]][:, :].unsqueeze(1),
                                          ALU.mult).then_inc(yc_ready, 1)
                    split_lo(U_CONV + 6 * m + s + 2, s % 2)
            apply(SPREAD[N_Q], AP_BASE[N_Q], [(zq[:, t, :], vcol[:, V_QG + t:V_QG + t + 1], None, cqh[:, t, :], cql[:, t, :])
                                      for t in range(QT)])
            dve.wait_ge(krh_ready, 1)
            dve.tensor_tensor(krl[:, :], pb[5][:, :], krh[:, :].bitcast(F32), ALU.subtract).then_inc(krl_ready, 1)

            def head_lo(h):
                b = h % 2
                dve.wait_ge(hi_ready, U_H + h + 1)
                src = raw[b][:, 0:QT * QH].rearrange("p (k f) -> p k f", k=QT)
                whf = wh[b][:, :].bitcast(F32)

                def part(t, lo_, hi_):
                    return t[:, lo_:hi_].rearrange("p (k f) -> p k f", k=QT)
                hi_n, hi_r = part(whf, 0, QT * P), part(whf, QT * P, 2 * QT * P)
                lo_n, lo_r = part(wl[b], 0, QT * P), part(wl[b], QT * P, 2 * QT * P)
                dve.tensor_tensor(lo_n, src[:, :, 0:128], hi_n, ALU.subtract)
                dve.tensor_tensor(lo_r[:, :, 0:64], src[:, :, 128:192], hi_r[:, :, 0:64], ALU.subtract)
                dve.tensor_tensor(lo_r[:, :, 64:96], src[:, :, 160:192], hi_r[:, :, 64:96], ALU.subtract)
                dve.tensor_tensor(lo_r[:, :, 96:128], src[:, :, 128:160], hi_r[:, :, 96:128], ALU.subtract)
                dve.tensor_tensor(wl[b][:, 768:1024], raw[b][:, QT * QH:QT * QH + 256], whf[:, 768:1024],
                                  ALU.subtract).then_inc(lo_ready, 1)

            def head_parts_lo(h):
                r = h % 2
                dve.wait_ge(ph_ready, 3 * h + 1)
                dve.tensor_tensor(qnl[:, r, :], pb[0][:, :], qnh[:, r, :].bitcast(F32), ALU.subtract).then_inc(pl_ready, 1)
                dve.wait_ge(q_done, 2 * h + 2)
                if h == 0:
                    dve.wait_ge(kr_dup, 1)
                else:
                    dve.wait_ge(pl_ready, 3 * h - 1)
                dve.tensor_tensor(rope[:, :], pb[1][:, :], cs[:, :], ALU.mult).then_inc(q_roped, 1)
                dve.wait_ge(ph_ready, 3 * h + 2)
                dve.wait_ge(q_roped, h + 1)
                dve.tensor_tensor(qrl[:, r, :], rope[:, :], qrh[:, r, :].bitcast(F32), ALU.subtract).then_inc(pl_ready, 1)
                dve.wait_ge(ph_ready, 3 * h + 3)
                dve.tensor_tensor(knl[:, r, :], pb[2][:, :], knh[:, r, :].bitcast(F32), ALU.subtract).then_inc(pl_ready, 1)

            def gained(y, src):
                return [(src, vcol[:, V_OUTG + y:V_OUTG + y + 1], None, hh[:, y, :], hl[:, y, :])]

            def apply_conv(j):
                apply(SPREAD_CONV + j, AP_CONV + j, gained(j, yc[:, j, :]))

            def apply_head(h):
                apply(SPREAD[N_HEAD + h], AP_BASE[N_HEAD] + h, gained(CT + h, o_raw[:, h, :]))

            def conv_inverse():
                dve.wait_ge(group_rms_ready, 1)
                dve.reciprocal(sq[:, 1, :], sq[:, 0, :]).then_inc(group_step, 1)
                dve.wait_ge(group_step, 1)
                dve.tensor_copy(group_rh[:, :], sq[:, 1, :]).then_inc(group_step, 1)
                dve.wait_ge(group_step, 2)
                dve.tensor_tensor(group_rl[:, :], sq[:, 1, :], group_rh[:, :].bitcast(F32), ALU.subtract).then_inc(group_r_ready, 1)

            def maximum(h, q):
                e, i = TT * h + q, TILE_OF[q]
                dve.wait_ge(s_done, e + 1)
                dve.tensor_reduce(nmax[:, e:e + 1], pb[3 + q % 2][:, 0:P * (i + 1)], AX_X, ALU.max,
                                  negate=True).then_inc(max_ready, 1)
                dve.wait_ge(max_ready, e + 1)
                dve.tensor_scalar(nmax_s[:, e:e + 1], nmax[:, e:e + 1], SCALE, None, ALU.mult).then_inc(nmax_ready, 1)

            def divide(h):
                sums = slice(TT * h, TT * (h + 1))
                dve.wait_ge(exp_ready, TT * (h + 1))
                dve.reciprocal(rinv[:, sums], rsum[:, sums]).then_inc(rinv_ready, 1)
                dve.wait_ge(rinv_ready, h + 1)
                for q in range(TT):
                    e, i = TT * h + q, TILE_OF[q]
                    pr = probs[:, h % 2, P_OFF[i]:P_OFF[i + 1]]
                    dve.tensor_scalar(pr, pr, rinv[:, e:e + 1], None, ALU.mult).then_inc(p_ready, 1)

            def turned_lo(h, q):
                i = TILE_OF[q]
                dve.wait_ge(pth_ready, TT * h + q + 1)
                dve.tensor_tensor(ptl[:, 0:i + 1, P * i:P * (i + 1)],
                                  turn_bank(h, q)[:, 0:P * (i + 1)].rearrange("p (k q) -> p k q", k=i + 1),
                                  pth[:, 0:i + 1, P * i:P * (i + 1)].bitcast(F32), ALU.subtract).then_inc(ptl_ready, 1)

            def maxima_and_turned(h):
                for q in range(TT):
                    maximum(h + 1, q)
                    turned_lo(h, q)

            def unit_lo(n):
                split_lo(n, n % 2)

            head_lo(0)
            for t in range(TT):
                dve.wait_ge(vh_ready, t + 1)
                dve.tensor_tensor(vl[:, t, :], pb[t][:, :], vh[:, t, :].bitcast(F32), ALU.subtract).then_inc(vl_ready, 1)
            head_lo(1)
            conv_inverse()
            head_parts_lo(0)
            head_lo(2)
            head_parts_lo(1)
            apply_conv(0)
            head_lo(3)
            for q in range(TT):
                maximum(0, q)
            divide(0)
            head_parts_lo(2)
            unit_lo(U_O)
            apply_conv(1)
            maxima_and_turned(0)
            divide(1)
            head_parts_lo(3)
            unit_lo(U_O + 1)
            apply_conv(2)
            maxima_and_turned(1)
            divide(2)
            apply_conv(3)
            inverse(N_HEAD)
            maxima_and_turned(2)
            divide(3)
            apply_head(0)
            unit_lo(U_O + 2)
            inverse(N_HEAD + 1)
            for q in range(TT):
                turned_lo(3, q)
            apply_head(1)
            unit_lo(U_O + 3)
            inverse(N_HEAD + 2)
            apply_head(2)
            unit_lo(U_O + 4)
            inverse(N_HEAD + 3)
            apply_head(3)
            dve.wait_ge(bc_done, SPREAD_CONV + CT)
            clear_sum(N_FFN2, N_Q)
            for o in range(3, len(O_UNITS)):
                upper, pair = O_UNITS[o]
                if upper:
                    for d in (2 * pair, 2 * pair + 1):
                        update(d, O_BANK[d], mods[:, 5 * DT + d:5 * DT + d + 1], U_O + o + 1, DT)
                unit_lo(U_O + o + 2)
                if upper:
                    for d in (2 * pair, 2 * pair + 1):
                        add_square(N_FFN2, SQ_BASE[N_FFN2] + d, (SQ_BASE[N_FFN2] + d) % 2)
            inverse(N_FFN2)
            apply_model(N_FFN2, 2, 6)

            with dve.Fori(0, FT) as i:
                up_tile(U_A2, 1, i)
            clear_sum(N_FINAL, N_FFN2)
            with dve.Fori(0, DT // 2 - 1) as m:
                down_pair(U_B2, 1, N_FINAL, 2 * DT, m)
            down_pair(U_B2, 1, N_FINAL, 2 * DT, DT // 2 - 1, 4)
            for k in range(0, DT, 2):
                dve.wait_ge(xg_turned, k + 1)
                dve.tensor_copy(o_nat[:, :, k * P:(k + 1) * P], pb[OUT_BANK[k % 4]][:, :].rearrange("p (t d) -> p t d", t=TT)).then_inc(o_moved[0], 1)
            inverse(N_FINAL, spread=False)
            for moved in o_moved:
                dve.wait_ge(moved, DT // 2)
            for t in range(TT):
                dve.tensor_scalar(o_nat[:, t, :], o_nat[:, t, :], rrms[:, t:t + 1], None, ALU.mult).then_inc(o_scaled, 1)


_INS = ["x", "c", "positions", "ada_w", "ada_b", "norm_ffn1_g", "ffn1_w1", "ffn1_w3", "ffn1_w2", "norm_mix_g",
        "w_in", "conv_w", "q_norm_g", "w_uq", "kv_norm_g", "w_ukv", "out_norm_g", "w_out", "norm_ffn2_g",
        "ffn2_w1", "ffn2_w3", "ffn2_w2", "final_norm_g"]


def _constants():
    import numpy as np
    k = np.zeros((P, K_ALL), np.float32)
    r = np.arange(P)
    k[:, K_IDENT:K_IDENT + P] = np.eye(P)
    k[:, K_DUP:K_DUP + P] = r[:, None] % QK_ROPE == r[None, :] % QK_ROPE
    k[:, K_DUP32:K_DUP32 + P] = r[:, None] % SQUARE == r[None, :] % SQUARE
    k[:, K_HALF] = r < P // 2
    k[:, K_HALF + 1] = r >= P // 2
    k[:, K_ONE] = 1.0
    ones, select, hidden = K_COLS, K_COLS + P, K_COLS + 2 * P
    k[:, ones:ones + P] = 1.0
    k[r % SQUARE == 0, select:select + P // 2] = 1.0
    k[r % SQUARE == 1, select + P // 2:select + P] = 1.0
    k[0, hidden + CHUNK:hidden + P] = -1e30
    inv = np.float32(ROPE_THETA) ** (-np.arange(0, QK_ROPE, 2, dtype=np.float32) / np.float32(QK_ROPE))
    k[:, K_ROPE] = inv[r % (QK_ROPE // 2)]
    k[:, K_ROPE + 1] = np.where(r < 64, 0.25, np.where(r < 96, 0.5, 0.0))
    k[:, K_ROPE + 2] = np.where(r < 64, np.pi / 2, np.where(r < 96, np.pi, 0.0))
    return k


def kernel(**inputs):
    import numpy as _np
    import concourse.bacc as _bacc
    from concourse import mybir as _mybir
    from concourse.bass_utils import run_bass_kernel_spmd as _run

    nc = _bacc.Bacc("TRN2", target_bir_lowering=False, num_devices=1)
    arrays, args = {}, []
    for name in _INS:
        a = _np.ascontiguousarray(inputs[name])
        arrays[f"in_{name}_dram"] = a
        args.append(nc.dram_tensor(f"in_{name}_dram", a.shape, _mybir.dt.from_np(a.dtype), kind="ExternalInput").ap())
    k = _constants()
    arrays["in_consts_dram"] = k
    args.append(nc.dram_tensor("in_consts_dram", k.shape, _mybir.dt.float32, kind="ExternalInput").ap())
    args.append(nc.dram_tensor("out_0_dram", (1, SEQ, D_MODEL), _mybir.dt.float32, kind="ExternalOutput").ap())
    hybrid_block(nc, *args)
    r = _run(nc, [arrays], core_ids=[0])
    return r.results[0]["out_0_dram"]
```

```python
from contextlib import ExitStack
import math

import concourse.bass as bass
from concourse import mybir

F32 = mybir.dt.float32
F32R = mybir.dt.float32r
I32 = mybir.dt.int32
ALU = mybir.AluOpType
ACT = mybir.ActivationFunctionType
AX_X = mybir.AxisListType.X

P = 128
D_MODEL, SEQ, D_FF, N_MOD = 1024, 512, 2816, 9
CONV_WIDTH, CONV_K, HEADS = 512, 3, 4
QK_NOPE, QK_ROPE, V_HEAD, Q_LORA, KV_LORA = 128, 64, 128, 384, 256
CHUNK, EPS, ROPE_THETA = 64, 1e-6, 10000.0
DT = D_MODEL // P
TT = SEQ // P
FT = D_FF // P
CT = CONV_WIDTH // P
QT, KT = Q_LORA // P, KV_LORA // P
UW = 1024
B_SPLIT = (8, 7, 7)
B_FROM = (0, 8, 15)
CQ0 = 3 * CONV_WIDTH
CKV0 = CQ0 + Q_LORA
KR0 = CKV0 + KV_LORA
QH = QK_NOPE + QK_ROPE
KVH = QK_NOPE + V_HEAD
SCALE = float(QH) ** -0.5

U_A1 = 0
U_B1 = U_A1 + 2 * FT
U_Z = U_B1 + 3 * DT
U_CONV = U_Z + QT + KT + 1
U_V = U_CONV + 3 * CT
U_H = U_V + KT
U_O = U_H + HEADS
U_A2 = U_O + DT
U_B2 = U_A2 + 2 * FT

N_FFN1, N_MIX, N_KV, N_Q, N_HEAD, N_FFN2, N_FINAL = 0, 1, 2, 3, 4, 8, 9
SQ_BASE = {N_FFN1: 0, N_MIX: 8, N_KV: 16, N_Q: 18, N_FFN2: 21, N_FINAL: 29}
SQ_TURN = {N_FFN1: 0, N_MIX: 1, N_KV: 2, N_Q: 3, N_FFN2: 4, N_FINAL: 5}
AP_BASE = {N_FFN1: 0, N_MIX: 8, N_KV: 16, N_Q: 18, N_HEAD: 25, N_FFN2: 29, N_FINAL: 37}
AP_CONV = 21
SPREAD = {N_FFN1: 0, N_MIX: 1, N_KV: 2, N_Q: 3, N_HEAD: 8, N_HEAD + 1: 9, N_HEAD + 2: 10, N_HEAD + 3: 11, N_FFN2: 12}
SPREAD_CONV = 4

K_IDENT, K_DUP, K_DUP32, K_HALF, K_ONE, K_ROPE = 0, 128, 256, 384, 416, 417
K_COLS = 420
K_ALL = K_COLS + 3 * P
SQUARE = 32
QUARTERS = P // SQUARE

V_ADAB, V_C, V_G1, V_GMIX, V_G2, V_GFIN = 0, 72, 80, 88, 96, 104
V_QG, V_KVG, V_OUTG, V_CONV = 112, 115, 117, 125
V_COLS, V_ROWS1 = 137, 112

TURN = 2.0 * math.pi
TURN1 = 6.28125
TURN2 = round((TURN - TURN1) * 2.0 ** 20) / 2.0 ** 20
TURN3 = TURN - TURN1 - TURN2
ROUND = 12582912.0
SIN_MAX = 3.1415925
ADA_PE = (2, 3)
ADA_START = 2 * DT - sum(ADA_PE)
LAG = 3
WARM_START, WARM_SQUARES, WARM_ROOT, WARM_NORMED, WARM_HEADS = 7, 16, 13, 16, 9
FREE = 1


def hybrid_block(nc, x, c, positions, ada_w, ada_b, norm_ffn1_g, ffn1_w1, ffn1_w3, ffn1_w2, norm_mix_g,
                 w_in, conv_w, q_norm_g, w_uq, kv_norm_g, w_ukv, out_norm_g, w_out, norm_ffn2_g,
                 ffn2_w1, ffn2_w3, ffn2_w2, final_norm_g, consts, out):
    with ExitStack() as ctx:
        def sem(name):
            return ctx.enter_context(nc.semaphore(name))

        top = [16512]

        def at(name, shape, dt=F32, offset=None):
            n = 4
            for s in shape[1:]:
                n *= s
            if offset is None:
                offset = top[0]
                top[0] += -(-n // 32) * 32
            return nc.alloc_sbuf_tensor_at(name, shape, dt, offset=offset)

        def place(base, *specs):
            made = []
            for name, shape, dt in specs:
                made.append(at(name, shape, dt, base))
                n = 4
                for s in shape[1:]:
                    n *= s
                base += n
            return made, base

        xres = at("xres", [P, DT, SEQ])
        hh_at = top[0]
        hh = at("hh", [P, DT, SEQ], F32R)
        hl_at = top[0]
        hl = at("hl", [P, DT, SEQ], F32R)
        raw = [at(f"raw{b}", [P, UW]) for b in range(2)]
        wh = [at(f"wh{b}", [P, UW], F32R) for b in range(2)]
        wl = [at(f"wl{b}", [P, UW], F32R) for b in range(2)]
        kst = at("kst", [P, K_COLS + 2])
        vcol = at("vcol", [P, V_COLS + 10])
        mods = at("mods", [P, N_MOD * DT])
        silu_c = at("silu_c", [P, DT])
        sig_c = at("sig_c", [P, DT])
        a_cols = at("a_cols", [P, 3, DT])
        half_gates = at("half_gates", [P, 2, DT])
        cs = at("cs", [P, SEQ])
        rms = at("rms", [P, TT])
        rrms = at("rrms", [P, TT])
        rrms_h = at("rrms_h", [P, TT], F32R)
        rrms_l = at("rrms_l", [P, TT])
        folded = at("folded", [P, D_MODEL // SQUARE])
        exact = at("exact", [P, 3, P], F32R)
        nmax_s = at("nmax_s", [P, HEADS * TT])
        nmax = at("nmax", [P, HEADS * TT])
        rsum = at("rsum", [P, HEADS * TT])
        rinv = at("rinv", [P, HEADS * TT])
        u_at = top[0]
        ubuf = at("ubuf", [P, 3, SEQ])
        (sigb, sbuf, gbuf), _ = place(u_at, ("sigb", [P, SEQ], F32), ("sbuf", [P, SEQ], F32), ("gbuf", [P, SEQ], F32))
        sq_at = top[0]
        sq = at("sq", [P, 2, SEQ])
        sacc = at("sacc", [P, SEQ])
        (group_rh, _, group_rl), _ = place(sq_at, ("group_rh", [P, SEQ], F32R), ("group_gap", [P, SEQ], F32),
                                           ("group_rl", [P, SEQ], F32R))
        diag_at = top[0]
        diag = at("diag", [P, 2, TT, P], F32R)
        (turned,), _ = place(diag_at, ("turned", [P, D_MODEL], F32))
        region = top[0]
        (gh, gl, ada_ring, acc), end = place(region, ("gh", [P, FT, SEQ], F32R), ("gl", [P, FT, SEQ], F32R),
                                             ("ada_ring", [P, 4, D_MODEL], F32), ("acc", [P, D_MODEL], F32))
        assert end <= 229344, end
        (ada_start, x_nat, vec1, vec2, kst2), e2 = place(region, ("ada_start", [P, 16, D_MODEL], F32),
                                                   ("x_nat", [P, TT, D_MODEL], F32), ("vec1", [P, P], F32),
                                                   ("vec2", [P, P], F32), ("kst2", [P, 3, P], F32))
        (pos, posf, ang, turns), e2 = place(e2, ("pos", [P, SEQ], I32), ("posf", [P, SEQ], F32),
                                            ("ang", [P, SEQ], F32), ("turns", [P, SEQ], F32))
        assert e2 <= end, e2
        (zkv, zq, ckh, ckl, cqh, cql), e3 = place(
            region, ("zkv", [P, KT, SEQ], F32), ("zq", [P, QT, SEQ], F32),
            ("ckh", [P, KT, SEQ], F32R), ("ckl", [P, KT, SEQ], F32R),
            ("cqh", [P, QT, SEQ], F32R), ("cql", [P, QT, SEQ], F32R))
        (o_raw,), _ = place(region, ("o_raw", [P, HEADS, SEQ], F32))
        (krh, krl, qnh, qnl, qrh, qrl, knh, knl, vh, vl), e3 = place(
            e3, ("krh", [P, SEQ], F32R), ("krl", [P, SEQ], F32R),
            ("qnh", [P, 2, SEQ], F32R), ("qnl", [P, 2, SEQ], F32R),
            ("qrh", [P, 2, SEQ], F32R), ("qrl", [P, 2, SEQ], F32R),
            ("knh", [P, 2, SEQ], F32R), ("knl", [P, 2, SEQ], F32R),
            ("vh", [P, TT, HEADS * V_HEAD], F32R), ("vl", [P, TT, HEADS * V_HEAD], F32R))
        (cbuf, ubufc, cacc), _ = place(e3, ("cbuf", [P, SEQ], F32), ("ubufc", [P, SEQ], F32), ("cacc", [P, SEQ], F32))
        (pth, ptl, yc, probs, gsq, rope), e3 = place(
            e3, ("pth", [P, TT, SEQ], F32R), ("ptl", [P, TT, SEQ], F32R), ("yc", [P, CT, SEQ], F32),
            ("probs", [P, 2, TT * (TT + 1) // 2 * P], F32), ("gsq", [P, SEQ], F32), ("rope", [P, SEQ], F32))
        assert e3 <= 229344, e3
        (xg,), _ = place(hh_at, ("xg", [P, DT, SEQ], F32))
        (o_nat,), _ = place(hl_at, ("o_nat", [P, TT, D_MODEL], F32))

        pb = [ctx.enter_context(nc.psum_tensor(f"pb{i}", [P, SEQ], F32)) for i in range(8)]
        norm_bank = pb[7]

        ident = kst[:, K_IDENT:K_IDENT + P]
        one_col = kst[:, K_ONE:K_ONE + 1]

        exact_landed, exact_ready = sem("exact_landed"), sem("exact_ready")
        consts_landed, vecs_landed, pos_landed, x_landed = sem("consts_landed"), sem("vecs_landed"), sem("pos_landed"), sem("x_landed")
        start_landed = [sem(f"start_landed{i}") for i in range(8)]
        ada_landed = [sem(f"ada_landed{i}") for i in range(4)]
        raw_landed = [sem("raw_landed0"), sem("raw_landed1")]
        kn_landed = [sem("kn_landed0"), sem("kn_landed1")]
        hi_ready, lo_ready, unit_done = sem("hi_ready"), sem("lo_ready"), sem("unit_done")
        vec_turned, vec_ready, sigc_ready, siluc_ready = sem("vec_turned"), sem("vec_ready"), sem("sigc_ready"), sem("siluc_ready")
        cs_step, cs_ready = sem("cs_step"), sem("cs_ready")
        x_turned, x_copied = sem("x_turned"), sem("x_copied")
        ada_turned, ada_folded, ada_summed = sem("ada_turned"), sem("ada_folded"), sem("ada_summed")
        ada_direct, mods_part = sem("ada_direct"), sem("mods_part")
        ada_step, mods_ready, cols_ready = sem("ada_step"), sem("mods_ready"), sem("cols_ready")
        sq_ready, sq_added, sacc_clear = sem("sq_ready"), sem("sq_added"), sem("sacc_clear")
        col_done, rms_ready, rrms_ready, diag_ready, bc_done = sem("col_done"), sem("rms_ready"), sem("rrms_ready"), sem("diag_ready"), sem("bc_done")
        rrms_split = sem("rrms_split")
        csq_ready, group_summed, group_rms_ready, group_step, group_r_ready = (
            sem("csq_ready"), sem("group_summed"), sem("group_rms_ready"), sem("group_step"), sem("group_r_ready"))
        u_ready, hh_ready, hl_ready = sem("u_ready"), sem("hh_ready"), sem("hl_ready")
        sig_ready, s_ready, g_ready, gh_ready, gl_ready = sem("sig_ready"), sem("s_ready"), sem("g_ready"), sem("gh_ready"), sem("gl_ready")
        x_upd = sem("x_upd")
        zkv_copied, zq_copied = sem("zkv_copied"), sem("zq_copied")
        kr_roped, kr_dup, krh_ready, krl_ready = sem("kr_roped"), sem("kr_dup"), sem("krh_ready"), sem("krl_ready")
        c_copied, u_conv, conv_step, yc_ready = sem("c_copied"), sem("u_conv"), sem("conv_step"), sem("yc_ready")
        vh_ready, vl_ready = sem("vh_ready"), sem("vl_ready")
        q_done, ph_ready, pl_ready, q_roped = sem("q_done"), sem("ph_ready"), sem("pl_ready"), sem("q_roped")
        s_done, max_ready, nmax_ready = sem("s_done"), sem("max_ready"), sem("nmax_ready")
        exp_ready, rinv_ready, p_ready = sem("exp_ready"), sem("rinv_ready"), sem("p_ready")
        t_done, pth_ready, ptl_ready = sem("t_done"), sem("pth_ready"), sem("ptl_ready")
        pv_done, o_copied, gsq_ready = sem("pv_done"), sem("o_copied"), sem("gsq_ready")
        xg_ready, xg_turned, out_stored = sem("xg_ready"), sem("xg_turned"), sem("out_stored")
        o_scaled = [sem("even_o_scaled"), sem("odd_o_scaled")]

        w1v = [w[0].rearrange("(k p) f -> p k f", p=P) for w in (ffn1_w1, ffn2_w1)]
        w3v = [w[0].rearrange("(k p) f -> p k f", p=P) for w in (ffn1_w3, ffn2_w3)]
        w2v = [w[0].rearrange("(k p) f -> p k f", p=P) for w in (ffn1_w2, ffn2_w2)]
        winv = w_in[0].rearrange("(k p) f -> p k f", p=P)
        woutv = w_out[0].rearrange("(k p) f -> p k f", p=P)
        wuqv = w_uq[0].rearrange("(k p) (h f) -> p k h f", p=P, h=HEADS)
        wukvv = w_ukv[0].rearrange("(k p) (h f) -> p k h f", p=P, h=HEADS)
        adav = ada_w[0].rearrange("(k p) f -> p k f", p=P)

        def z_tile(i):
            return CONV_WIDTH + i * P, 2 * CONV_WIDTH + i * P, i * P

        def cols(t, k, n=P):
            return t[:, k * n:(k + 1) * n]

        CONV_BANKS = ((0, 1, 2), (3, 4, 6))
        OUT_BANK = (0, 1, 4, 5, 6, 2, 3, 0)
        HALF = DT // 2
        O_BANK = (0, 1, 2, 3, 4, 5, 0, 1)
        O_UNITS = ((0, 0), (0, 1), (0, 2), (1, 0), (1, 1), (1, 2), (0, 3), (1, 3))
        P_OFF = [P * i * (i + 1) // 2 for i in range(TT + 1)]

        TILE_OF = tuple(reversed(range(TT)))

        def turn_bank(h, q):
            return pb[5 + (5 * h + q) % 2]

        block = ctx.enter_context(nc.Block())

        @block.sync
        def _(sp):
            sp.dma_start(kst[:, 0:K_COLS], consts[:, 0:K_COLS]).then_inc(consts_landed, 16)
            sp.dma_start(pos[:, :], positions.partition_broadcast(P).rearrange("p a s -> p (a s)")).then_inc(pos_landed, 16)
            sp.dma_start(x_nat[:, :, :], x[0].rearrange("(t p) d -> p t d", p=P)).then_inc(x_landed, 16)
            row = 0
            for v, n in ((ada_b, 72), (c, 8), (norm_ffn1_g, 8), (norm_mix_g, 8), (norm_ffn2_g, 8)):
                sp.dma_start(vec1[row:row + n, :], v[0].rearrange("(r q) -> r q", q=P)).then_inc(vecs_landed, 16)
                row += n
            sp.dma_start(vec1[row:row + 8, :], final_norm_g.rearrange("(r q) -> r q", q=P)).then_inc(vecs_landed, 16)
            row = 0
            for v, n in ((q_norm_g, QT), (kv_norm_g, KT), (out_norm_g, DT)):
                sp.dma_start(vec2[row:row + n, :], v[0].rearrange("(r q) -> r q", q=P)).then_inc(vecs_landed, 16)
                row += n
            sp.dma_start(vec2[row:row + CONV_K * CT, :],
                         conv_w[0].rearrange("t (r q) -> (t r) q", q=P)).then_inc(vecs_landed, 16)
            sp.dma_start(kst2[:, :, :], consts[:, K_COLS:K_ALL].rearrange("p (a b) -> p a b", a=3)).then_inc(exact_landed, 16)

            def start_load(i):
                col = D_MODEL if i < 4 else 0
                k = 2 * (i % 4)
                sp.dma_start(ada_start[:, 2 * i:2 * i + 2, :], adav[:, k:k + 2, col:col + D_MODEL]).then_inc(start_landed[i], 16)

            def load(n, par, src, width=UW):
                if not isinstance(n, int) or n > 2:
                    sp.wait_ge(lo_ready, n - 1)
                shape = list(src.shape)[1:]
                dst = raw[par][:, 0:width]
                if len(shape) == 2:
                    dst = dst.rearrange("p (k f) -> p k f", k=shape[0])
                sp.dma_start(dst, src).then_inc(raw_landed[par], 16)

            def up_units(base, f, i):
                col = sp.snap(i * P)
                load(base + 2 * i, 0, w1v[f][:, :, bass.ds(col, P)])
                load(base + 2 * i + 1, 1, w3v[f][:, :, bass.ds(col, P)])

            def down_units(base, f):
                with sp.Fori(0, DT // 2) as m:
                    for s in range(6):
                        p, kk = divmod(s, 3)
                        k0, n = B_FROM[kk], B_SPLIT[kk]
                        col = sp.snap(m * (2 * P) + p * P)
                        load(base + 6 * m + s, s % 2, w2v[f][:, k0:k0 + n, bass.ds(col, P)], n * P)

            for i in range(4):
                start_load(i)
            for i in range(4, 8):
                start_load(i)
            sp.dma_start(raw[0].rearrange("p (k f) -> p k f", k=DT), w1v[0][:, :, 0:P]).then_inc(raw_landed[0], 16)
            sp.dma_start(raw[1].rearrange("p (k f) -> p k f", k=DT), w3v[0][:, :, 0:P]).then_inc(raw_landed[1], 16)
            with sp.Fori(1, FT) as i:
                up_units(U_A1, 0, i)
            down_units(U_B1, 0)
            for j, c0 in enumerate([CKV0 + P * t for t in range(KT)] + [CQ0 + P * t for t in range(QT)]):
                load(U_Z + j, j % 2, winv[:, :, c0:c0 + P])
            load(U_Z + KT + QT, 1, winv[:, :, KR0:KR0 + QK_ROPE], DT * QK_ROPE)
            with sp.Fori(1, CT // 2 + 1) as m:
                for s in range(6):
                    p, which = divmod(s, 3)
                    c0 = z_tile(p)[which] - 2 * P
                    load(U_CONV - 6 + 6 * m + s, s % 2, winv[:, :, bass.ds(m * (2 * P) + c0, P)])
            for k in range(KT):
                load(U_V + k, k % 2, wukvv[:, k, :, QK_NOPE:KVH], HEADS * V_HEAD)
            for h in range(HEADS):
                load(U_H + h, h % 2, wuqv[:, :, h, :], QT * QH)
                sp.dma_start(raw[h % 2][:, QT * QH:QT * QH + KT * QK_NOPE].rearrange("p (k f) -> p k f", k=KT),
                             wukvv[:, :, h, 0:QK_NOPE]).then_inc(kn_landed[h % 2], 16)
            for o, (upper, pair) in enumerate(O_UNITS):
                load(U_O + o, o % 2, woutv[:, 4 * upper:4 * upper + 4, 2 * P * pair:2 * P * (pair + 1)])
            with sp.Fori(0, FT) as i:
                up_units(U_A2, 1, i)
            down_units(U_B2, 1)
            outv = out[0].rearrange("(t p) d -> p t d", p=P)
            for g in range(DT):
                half, t = divmod(g, TT)
                sp.wait_ge(o_scaled[g % 2], g // 2 + 1)
                sp.dma_start(outv[:, t, half * SEQ:(half + 1) * SEQ], o_nat[:, t, half * SEQ:(half + 1) * SEQ]).then_inc(out_stored, 16)
            sp.wait_ge(out_stored, 16 * DT)

        @block.gpsimd
        def _(pool):
            pool.wait_ge(sacc_clear, 1)
            for k in range(DT):
                pool.wait_ge(sq_ready, k + 1)
                pool.wait_ge(sq_added, k)
                pool.tensor_tensor(sacc[:, :], sacc[:, :], sq[:, k % 2, :], ALU.add).then_inc(sq_added, 1)
            for n in range(2):
                pool.wait_ge(hi_ready, n + 1)
                pool.tensor_tensor(wl[n][:, :], raw[n][:, :], wh[n][:, :].bitcast(F32), ALU.subtract).then_inc(lo_ready, 1)
            pool.wait_ge(mods_ready, 2)
            with pool.Fori(0, N_MOD - 2) as j:
                for k in range(DT):
                    pool.wait_ge(ada_step, ADA_START + j * DT + k - 3)
                    pool.dma_start(ada_ring[:, k % 4, :], adav[:, k, bass.ds(j * D_MODEL + 2 * D_MODEL, D_MODEL)]) \
                        .then_inc(ada_landed[k % 4], 16)

            def unit_lo(n):
                pool.wait_ge(hi_ready, n + 1)
                pool.wait_ge(lo_ready, n)
                pool.tensor_tensor(wl[n % 2][:, :], raw[n % 2][:, :], wh[n % 2][:, :].bitcast(F32),
                                   ALU.subtract).then_inc(lo_ready, 1)

            def conv_lo(j):
                idx = AP_CONV + j
                pool.wait_ge(hh_ready, idx + 1)
                pool.wait_ge(hl_ready, idx)
                pool.tensor_tensor(hl[:, j, :], ubuf[:, idx % 3, :], hh[:, j, :].bitcast(F32), ALU.subtract).then_inc(hl_ready, 1)

            conv_lo(0)
            unit_lo(U_O)
            conv_lo(1)
            conv_lo(2)
            unit_lo(U_O + 1)
            conv_lo(3)
            unit_lo(U_O + 2)
            unit_lo(U_O + 3)
            unit_lo(U_O + 4)

        @block.scalar
        def _(act):
            def split_hi(n, par, landed):
                act.wait_ge(raw_landed[par], landed)
                if not isinstance(n, int) or n >= 2:
                    act.wait_ge(unit_done, n - 1)
                act.activation(wh[par][:, :], raw[par][:, :], ACT.Copy).then_inc(hi_ready, 1)

            def landed(n):
                return 16 * (n // 2 + 1)

            def square(idx, slot, src):
                if not isinstance(idx, int) or idx >= 2:
                    act.wait_ge(sq_added, idx - 1)
                act.activation(sq[:, slot, :], src, ACT.Square).then_inc(sq_ready, 1)

            def root(n, width):
                act.wait_ge(col_done, n + 1)
                act.activation(rms[:, :], norm_bank[:, 0:TT], ACT.Sqrt, scale=1.0 / width,
                               bias=kst[:, K_COLS:K_COLS + 1]).then_inc(rms_ready, 1)

            def sqrt_table(spare):
                act.activation(vcol[:, V_COLS + spare:V_COLS + spare + 1], kst[:, K_COLS:K_COLS + 1], ACT.Sqrt)

            def norm_hi(idx, dst, shift=None):
                act.wait_ge(u_ready, idx + 1)
                if shift is None:
                    act.activation(dst, ubuf[:, idx % 3, :], ACT.Copy).then_inc(hh_ready, 1)
                else:
                    act.activation(dst, ubuf[:, idx % 3, :], ACT.Identity, bias=shift).then_inc(hh_ready, 1)

            def norm_model(n, shift_mod):
                for k in range(DT):
                    s = shift_mod * DT + k
                    norm_hi(AP_BASE[n] + k, hh[:, k, :], mods[:, s:s + 1])

            def up(base, f):
                with act.Fori(0, FT) as i:
                    act.activation(vcol[:, V_COLS + 9:V_COLS + 10], kst[:, K_COLS:K_COLS + 1], ACT.Sigmoid)
                    split_hi(base + 2 * i + 2, 0, 16 * i + landed(base + 2))
                    act.wait_ge(unit_done, base + 2 * i + 1)
                    act.wait_ge(s_ready, FREE + f * FT + i)
                    act.activation(sigb[:, :], pb[0][:, :], ACT.Sigmoid).then_inc(sig_ready, 1)
                    split_hi(base + 2 * i + 3, 1, 16 * i + landed(base + 2))
                    act.wait_ge(g_ready, FREE + f * FT + i + 1)
                    act.activation(gh[:, bass.ds(i, 1), :], gbuf[:, :].unsqueeze(1), ACT.Copy).then_inc(gh_ready, 1)

            def down(base, n, upd, final=False):
                with act.Fori(0, DT // 2) as m:
                    for s in range(6):
                        p, kk = divmod(s, 3)
                        if kk == 2:
                            act.wait_ge(x_upd, upd + 2 * m + p + 1)
                            square(SQ_BASE[n] + 2 * m + p, (SQ_BASE[n] + p) % 2, xres[:, bass.ds(2 * m + p, 1), :])
                        split_hi(base + 6 * m + s + 2, s % 2, 48 * m + landed(base + s + 2))

            act.wait_ge(vec_ready, 3)
            act.activation(sig_c[:, :], vcol[:, V_C:V_C + DT], ACT.Sigmoid).then_inc(sigc_ready, 1)
            act.wait_ge(cs_step, 10)
            act.activation(cs[:, :], ang[:, :], ACT.Sin).then_inc(cs_ready, 1)
            for k in range(DT):
                act.wait_ge(x_turned, k + 1)
                act.activation(xres[:, k, :], pb[k % 4][:, :], ACT.Copy).then_inc(x_copied, 1)
                act.wait_ge(x_copied, k + 1)
                square(k, k % 2, xres[:, k, :])
            sqrt_table(6)
            root(N_FFN1, D_MODEL)
            act.wait_ge(exact_landed, 16)
            act.activation(exact[:, :, :], kst2[:, :, :], ACT.Copy).then_inc(exact_ready, 1)
            split_hi(0, 0, 16)
            split_hi(1, 1, 16)
            act.wait_ge(mods_ready, 2)
            norm_model(N_FFN1, 0)

            up(U_A1, 0)
            sqrt_table(7)
            down(U_B1, N_MIX, 0)

            root(N_MIX, D_MODEL)
            norm_model(N_MIX, 3)
            for j in range(KT + QT + 1):
                n = U_Z + j + 2
                if j + 2 == KT + QT:
                    act.wait_ge(raw_landed[1], landed(n))
                    act.wait_ge(unit_done, n - 1)
                    src = raw[1][:, 0:DT * QK_ROPE].rearrange("p (k f) -> p k f", k=DT)
                    dst = wh[1].rearrange("p (k f) -> p k f", k=DT)
                    act.activation(dst[:, :, 0:64], src, ACT.Copy)
                    act.activation(dst[:, :, 64:96], src[:, :, 32:64], ACT.Copy)
                    act.activation(dst[:, :, 96:128], src[:, :, 0:32], ACT.Copy).then_inc(hi_ready, 1)
                else:
                    split_hi(n, n % 2, landed(n))
                act.wait_ge(unit_done, U_Z + j + 1)
                if j < KT:
                    act.activation(zkv[:, j, :], pb[j][:, :], ACT.Copy).then_inc(zkv_copied, 1)
                    act.wait_ge(zkv_copied, j + 1)
                    square(SQ_BASE[N_KV] + j, (SQ_BASE[N_KV] + j) % 2, zkv[:, j, :])
                elif j < KT + QT:
                    q = j - KT
                    act.activation(zq[:, q, :], pb[j][:, :], ACT.Copy).then_inc(zq_copied, 1)
                    act.wait_ge(zq_copied, q + 1)
                    square(SQ_BASE[N_Q] + q, (SQ_BASE[N_Q] + q) % 2, zq[:, q, :])
                if j == KT:
                    root(N_KV, KV_LORA)
                if j == KT + 1:
                    for t in range(KT):
                        norm_hi(AP_BASE[N_KV] + t, ckh[:, t, :])
            root(N_Q, Q_LORA)
            with act.Fori(0, CT // 2) as m:
                for s in range(6):
                    p, which = divmod(s, 3)
                    if which == 0:
                        act.wait_ge(unit_done, U_CONV + 6 * m + s + 1)
                        act.wait_ge(u_conv, FREE + 2 * m + p)
                        act.activation(cbuf[:, :], pb[CONV_BANKS[p][0]][:, :], ACT.Copy).then_inc(c_copied, 1)
                    split_hi(U_CONV + 6 * m + s + 2, s % 2, 48 * m + landed(U_CONV + s + 2))
            def conv_square(j):
                act.wait_ge(yc_ready, FREE + j + 1)
                act.wait_ge(sq_added, SQ_BASE[N_Q] + QT)
                if j >= 2:
                    act.wait_ge(group_summed, j - 1)
                act.activation(sq[:, j % 2, :], yc[:, j, :], ACT.Square).then_inc(csq_ready, 1)

            conv_square(0)
            conv_square(1)
            for t in range(QT):
                norm_hi(AP_BASE[N_Q] + t, cqh[:, t, :])

            def head_square(h):
                if h >= 1:
                    act.wait_ge(col_done, N_HEAD + h)
                act.activation(gsq[:, :], o_raw[:, h, :], ACT.Square).then_inc(gsq_ready, 1)

            def head_hi(h):
                b = h % 2
                n = U_H + h
                act.wait_ge(raw_landed[b], landed(n))
                act.wait_ge(kn_landed[b], 16 * (h // 2 + 1))
                act.wait_ge(unit_done, n - 1)
                src = raw[b][:, 0:QT * QH].rearrange("p (k f) -> p k f", k=QT)
                nope = wh[b][:, 0:QT * P].rearrange("p (k f) -> p k f", k=QT)
                rp = wh[b][:, QT * P:2 * QT * P].rearrange("p (k f) -> p k f", k=QT)
                act.activation(nope, src[:, :, 0:QK_NOPE], ACT.Copy)
                act.activation(rp[:, :, 0:64], src[:, :, 128:192], ACT.Copy)
                act.activation(rp[:, :, 64:96], src[:, :, 160:192], ACT.Copy)
                act.activation(rp[:, :, 96:128], src[:, :, 128:160], ACT.Copy)
                act.activation(wh[b][:, 768:1024], raw[b][:, QT * QH:QT * QH + 256], ACT.Copy).then_inc(hi_ready, 1)

            def head_parts_hi(h, after_first=None):
                r = h % 2
                if h >= 2:
                    act.wait_ge(s_done, 4 * (h - 1))
                act.wait_ge(q_done, 2 * h + 1)
                act.activation(qnh[:, r, :], pb[0][:, :], ACT.Copy).then_inc(ph_ready, 1)
                if after_first is not None:
                    after_first()
                act.wait_ge(q_roped, h + 1)
                act.activation(qrh[:, r, :], rope[:, :], ACT.Copy).then_inc(ph_ready, 1)
                act.wait_ge(unit_done, U_H + h + 1)
                act.activation(knh[:, r, :], pb[2][:, :], ACT.Copy).then_inc(ph_ready, 1)

            def exp(h, q):
                e, i = TT * h + q, TILE_OF[q]
                act.wait_ge(nmax_ready, e + 1)
                if h >= 2:
                    act.wait_ge(t_done, TT * (h - 2) + q + 1)
                act.activation(probs[:, h % 2, P_OFF[i]:P_OFF[i + 1]], pb[3 + q % 2][:, 0:P * (i + 1)], ACT.Exp,
                               scale=SCALE, bias=nmax_s[:, e:e + 1], accum_out=rsum[:, e:e + 1]).then_inc(exp_ready, 1)

            def turned_hi(h, q):
                i = TILE_OF[q]
                act.wait_ge(t_done, TT * h + q + 1)
                act.wait_ge(pv_done, h)
                act.activation(pth[:, 0:i + 1, P * i:P * (i + 1)],
                               turn_bank(h, q)[:, 0:P * (i + 1)].rearrange("p (k q) -> p k q", k=i + 1),
                               ACT.Copy).then_inc(pth_ready, 1)

            def exps_and_turned(h, behind=None):
                for q in range(TT):
                    turned_hi(h, q)
                    exp(h + 1, q)
                    if behind is not None and q in behind:
                        behind[q]()

            def head_out(h):
                act.wait_ge(pv_done, h + 1)
                act.activation(o_raw[:, h, :], turn_bank(h, 4)[:, :], ACT.Copy).then_inc(o_copied, 1)
                act.wait_ge(o_copied, h + 1)

            def unit_hi(n):
                split_hi(n, n % 2, landed(n))

            def conv_hi(j):
                norm_hi(AP_CONV + j, hh[:, j, :])

            def head_norm_hi(h):
                norm_hi(AP_BASE[N_HEAD] + h, hh[:, CT + h, :])

            head_hi(0)
            for t in range(TT):
                act.wait_ge(unit_done, U_V + KT)
                act.activation(vh[:, t, :], pb[t][:, :], ACT.Copy).then_inc(vh_ready, 1)
            conv_square(2)
            act.wait_ge(kr_dup, 1)
            act.activation(krh[:, :], pb[5][:, :], ACT.Copy).then_inc(krh_ready, 1)
            conv_square(3)
            head_hi(1)
            def conv_root():
                act.wait_ge(group_summed, CT)
                act.activation(sq[:, 0, :], pb[4][:, :], ACT.Sqrt, scale=1.0 / (CONV_WIDTH // 8),
                               bias=kst[:, K_COLS:K_COLS + 1]).then_inc(group_rms_ready, 1)

            head_parts_hi(0, conv_root)
            head_hi(2)
            head_parts_hi(1)
            exp(0, 0)
            exp(0, 1)
            head_hi(3)
            exp(0, 2)
            exp(0, 3)
            exps_and_turned(0)
            head_parts_hi(2)
            unit_hi(U_O)
            head_out(0)
            head_square(0)
            head_parts_hi(3)
            exps_and_turned(1, {0: lambda: conv_hi(0), 2: lambda: conv_hi(1), 3: lambda: conv_hi(2)})
            unit_hi(U_O + 1)
            head_out(1)
            conv_hi(3)
            root(N_HEAD, V_HEAD)
            head_square(1)
            exps_and_turned(2)
            head_norm_hi(0)
            head_out(2)
            for q in range(TT):
                turned_hi(3, q)
            unit_hi(U_O + 2)
            root(N_HEAD + 1, V_HEAD)
            head_square(2)
            unit_hi(U_O + 3)
            head_norm_hi(1)
            head_out(3)
            root(N_HEAD + 2, V_HEAD)
            head_square(3)
            unit_hi(U_O + 4)
            head_norm_hi(2)
            root(N_HEAD + 3, V_HEAD)
            head_norm_hi(3)
            for o in range(3, len(O_UNITS)):
                upper, pair = O_UNITS[o]
                last = o == len(O_UNITS) - 1
                if not last:
                    unit_hi(U_O + o + 2)
                if upper:
                    for d in (2 * pair, 2 * pair + 1):
                        act.wait_ge(x_upd, DT + d + 1)
                        square(SQ_BASE[N_FFN2] + d, (SQ_BASE[N_FFN2] + d) % 2, xres[:, d, :])
                if last:
                    unit_hi(U_O + o + 2)
            root(N_FFN2, D_MODEL)
            norm_model(N_FFN2, 6)

            up(U_A2, 1)
            sqrt_table(8)
            with act.Fori(0, DT // 2 - 1) as m:
                for s in range(6):
                    p, kk = divmod(s, 3)
                    if kk == 2:
                        act.wait_ge(x_upd, 2 * DT + 2 * m + p + 1)
                        square(SQ_BASE[N_FINAL] + 2 * m + p, (SQ_BASE[N_FINAL] + p) % 2, xres[:, bass.ds(2 * m + p, 1), :])
                    split_hi(U_B2 + 6 * m + s + 2, s % 2, 48 * m + landed(U_B2 + s + 2))
                    if kk == 2:
                        act.activation(xg[:, bass.ds(2 * m + p, 1), :], xres[:, bass.ds(2 * m + p, 1), :], ACT.Copy,
                                       scale=vcol[:, bass.ds(2 * m + p + V_GFIN, 1)]).then_inc(xg_ready, 1)
            for s in range(6):
                p, kk = divmod(s, 3)
                d = DT - 2 + p
                if s < 4:
                    n = U_B2 + 3 * (DT - 2) + s + 2
                    split_hi(n, n % 2, landed(n))
                if kk == 2:
                    act.wait_ge(x_upd, 2 * DT + d + 1)
                    square(SQ_BASE[N_FINAL] + d, (SQ_BASE[N_FINAL] + d) % 2, xres[:, d, :])
                    act.activation(xg[:, d, :], xres[:, d, :], ACT.Copy, scale=vcol[:, V_GFIN + d:V_GFIN + d + 1]).then_inc(xg_ready, 1)
            root(N_FINAL, D_MODEL)
            act.wait_ge(rrms_ready, N_FINAL + 1)
            for g in range(1, DT, 2):
                half, t = divmod(g, TT)
                act.wait_ge(xg_turned, g + 1)
                act.activation(o_nat[:, t, half * SEQ:(half + 1) * SEQ], pb[OUT_BANK[g]][:, :], ACT.Copy,
                               scale=rrms[:, t:t + 1]).then_inc(o_scaled[1], 1)

        @block.tensor
        def _(pe):
            def three(o, pairs, start, stop, check=False):
                last = None
                for j, (sh, sl, mh, ml) in enumerate(pairs):
                    for t, (a, b) in enumerate(((sh, mh), (sh, ml), (sl, mh))):
                        last = pe.matmul(o, a, b, start=start and j == 0 and t == 0,
                                         stop=stop and j == len(pairs) - 1 and t == 2)
                return last

            def unit(n):
                pe.wait_ge(lo_ready, n + 1)

            def h_product(o, b, hbase):
                for k in range(DT):
                    pe.wait_ge(hl_ready, hbase + k + 1)
                    last = three(o, [(cols(wh[b], k), cols(wl[b], k), hh[:, k, :], hl[:, k, :])], k == 0, k == DT - 1)
                return last

            def norm_sum(n, src, applied):
                if n >= 1:
                    pe.wait_ge(u_ready, applied)
                for t in range(TT):
                    last = pe.matmul(norm_bank[:, t:t + 1], src[:, t * P:(t + 1) * P], one_col, start=True, stop=True)
                last.then_inc(col_done, 1)

            def norm_spread(n):
                for part in range(2):
                    pe.wait_ge(diag_ready, 2 * n + part + 1)
                    last = pe.matmul(norm_bank[:, :], exact[:, 0, :], diag[:, part, :, :], start=part == 0, stop=part == 1)
                last.then_inc(bc_done, 1)

            def warm(n, bank=6):
                for _ in range(n):
                    pe.matmul(pb[bank][:, 0:3 * P], exact[:, 0, :], exact[:, :, :], start=True, stop=True)

            def first_pair(base, hbase):
                for k in range(DT + LAG):
                    for b, kb in ((0, k), (1, k - LAG)):
                        if not 0 <= kb < DT:
                            continue
                        if kb == 0:
                            unit(base + b)
                        pe.wait_ge(hl_ready, hbase + kb + 1)
                        last = three(pb[b][:, :], [(cols(wh[b], kb), cols(wl[b], kb), hh[:, kb, :], hl[:, kb, :])],
                                     kb == 0, kb == DT - 1)
                        if kb == DT - 1:
                            last.then_inc(unit_done, 1)

            def up_tile(base, f, i, n_norm):
                unit(base + 2 * i)
                pe.wait_ge(s_ready, FREE + f * FT + i)
                h_product(pb[0][:, :], 0, AP_BASE[n_norm]).then_inc(unit_done, 1)
                unit(base + 2 * i + 1)
                pe.wait_ge(g_ready, FREE + f * FT + i)
                h_product(pb[1][:, :], 1, AP_BASE[n_norm]).then_inc(unit_done, 1)

            def down(base, f, n_norm):
                with pe.Fori(0, DT // 2) as m:
                    for s in range(6):
                        p, kk = divmod(s, 3)
                        b = s % 2
                        unit(base + 6 * m + s)
                        if kk == 0:
                            pe.wait_ge(sq_added, SQ_BASE[n_norm] + 2 * m + p - 1)
                        for j in range(B_SPLIT[kk]):
                            k = B_FROM[kk] + j
                            pe.wait_ge(gl_ready, FREE + f * FT + k + 1)
                            last = three(pb[2 + p][:, :], [(cols(wh[b], j), cols(wl[b], j), gh[:, k, :], gl[:, k, :])],
                                         k == 0, k == FT - 1)
                        last.then_inc(unit_done, 1)

            pe.wait_ge(consts_landed, 16)
            pe.wait_ge(vecs_landed, 16 * 10)
            pe.transpose(pb[4][:, 0:V_ROWS1], vec1[0:V_ROWS1, :], ident[0:V_ROWS1, 0:V_ROWS1]).then_inc(vec_turned, 1)
            pe.transpose(pb[5][:, 0:V_COLS - V_ROWS1], vec2[0:V_COLS - V_ROWS1, :],
                         ident[0:V_COLS - V_ROWS1, 0:V_COLS - V_ROWS1]).then_inc(vec_turned, 1)
            pe.wait_ge(x_landed, 16)
            for k in range(DT):
                if k >= 4:
                    pe.wait_ge(x_copied, k - 3)
                for t in range(TT):
                    last = pe.transpose(pb[k % 4][:, t * P:(t + 1) * P], x_nat[:, t, k * P:(k + 1) * P], ident)
                last.then_inc(x_turned, 1)

            def ada_columns(v):
                n = ADA_PE[v]
                for pair in range(-(-n // 2)):
                    pe.wait_ge(start_landed[4 * v + pair], 16)
                for col in range(DT):
                    for k in range(n):
                        last = pe.matmul(pb[5 + v][:, col:col + 1], ada_start[:, DT * v + k, col * P:(col + 1) * P],
                                         silu_c[:, k:k + 1], start=k == 0, stop=k == n - 1)
                last.then_inc(ada_direct, 1)

            pe.wait_ge(siluc_ready, 1)
            ada_columns(0)
            pe.wait_ge(sq_added, DT)
            norm_sum(N_FFN1, sacc, 0)

            def mod_columns(v):
                pe.wait_ge(ada_folded, v + 1)
                pe.wait_ge(mods_ready, v)
                pe.matmul(pb[4][:, 0:D_MODEL // SQUARE], kst[:, K_DUP32:K_DUP32 + P], folded[:, :],
                          start=True, stop=True).then_inc(ada_summed, 1)

            pe.wait_ge(vec_ready, 1)
            mod_columns(0)
            pe.wait_ge(exact_ready, 1)
            norm_spread(N_FFN1)
            ada_columns(1)
            warm(WARM_START, 3)
            mod_columns(1)
            warm(WARM_START, 3)

            first_pair(U_A1, AP_BASE[N_FFN1])
            with pe.Fori(0, (FT - 1) // 3) as j:
                for t in range(3):
                    up_tile(U_A1, 0, 3 * j + t + 1, N_FFN1)
                mod_columns(j + 2)
            down(U_B1, 0, N_MIX)
            warm(WARM_SQUARES)
            pe.wait_ge(sq_added, SQ_BASE[N_MIX] + DT)
            norm_sum(N_MIX, sacc, AP_BASE[N_MIX])
            warm(WARM_ROOT)
            norm_spread(N_MIX)
            warm(WARM_NORMED)

            first_pair(U_Z, AP_BASE[N_MIX])
            for j in range(2, KT + QT + 1):
                unit(U_Z + j)
                h_product(pb[j][:, :], j % 2, AP_BASE[N_MIX]).then_inc(unit_done, 1)
                if j == KT:
                    pe.wait_ge(sq_added, SQ_BASE[N_KV] + KT)
                    norm_sum(N_KV, sacc, AP_BASE[N_KV])
                if j == KT + 1:
                    norm_spread(N_KV)
            pe.wait_ge(sq_added, SQ_BASE[N_Q] + QT)
            norm_sum(N_Q, sacc, AP_BASE[N_Q])
            with pe.Fori(0, CT // 2) as m:
                for s in range(6):
                    p, which = divmod(s, 3)
                    unit(U_CONV + 6 * m + s)
                    if which == 2:
                        pe.wait_ge(yc_ready, FREE + 2 * m + p)
                    h_product(pb[CONV_BANKS[p][which]][:, :], s % 2, AP_BASE[N_MIX]).then_inc(unit_done, 1)
            norm_spread(N_Q)
            pe.wait_ge(kr_roped, 1)
            pe.matmul(pb[5][:, :], kst[:, K_DUP:K_DUP + P], rope[:, :], start=True, stop=True).then_inc(kr_dup, 1)

            def v_unit(k):
                unit(U_V + k)
                if k == 0:
                    pe.wait_ge(yc_ready, FREE + CT)
                for t in range(TT):
                    last = three(pb[t][:, :], [(ckh[:, k, t * P:(t + 1) * P], ckl[:, k, t * P:(t + 1) * P],
                                                wh[k % 2][:, 0:HEADS * V_HEAD], wl[k % 2][:, 0:HEADS * V_HEAD])],
                                 k == 0, k == KT - 1)
                last.then_inc(unit_done, 1)

            def head_part(h, part):
                b = h % 2
                if part == 0:
                    unit(U_H + h)
                    pe.wait_ge(hl_ready, AP_BASE[N_Q] + QT)
                if h == 0:
                    pe.wait_ge(vl_ready, part + 1)
                elif part == 1:
                    pe.wait_ge(q_roped, h)
                else:
                    pe.wait_ge(pl_ready, 3 * (h - 1) + part + 1)
                if part < 2:
                    three(pb[part][:, :], [(cols(wh[b], QT * part + k), cols(wl[b], QT * part + k), cqh[:, k, :], cql[:, k, :])
                                           for k in range(QT)], True, True).then_inc(q_done, 1)
                else:
                    three(pb[2][:, :], [(cols(wh[b], 2 * QT + k), cols(wl[b], 2 * QT + k), ckh[:, k, :], ckl[:, k, :])
                                        for k in range(KT)], True, True).then_inc(unit_done, 1)

            def head_unit(h):
                for part in range(3):
                    head_part(h, part)

            def conv_sum(j):
                pe.wait_ge(csq_ready, j + 1)
                if j == 0:
                    pe.wait_ge(u_conv, FREE + CT)
                pe.matmul(pb[4][SQUARE * j:SQUARE * (j + 1), :], kst[:, K_HALF:K_HALF + SQUARE], sq[:, j % 2, :],
                          start=True, stop=True).then_inc(group_summed, 1)

            def conv_spread(j):
                rows = slice(SQUARE * j, SQUARE * (j + 1))
                pe.wait_ge(group_r_ready, 1)
                pe.wait_ge(u_ready, AP_CONV + j)
                pe.matmul(norm_bank[:, :], exact[rows, 1, :], group_rh[rows, :], start=True, stop=False)
                pe.matmul(norm_bank[:, :], exact[rows, 1, :], group_rl[rows, :], start=False, stop=True).then_inc(bc_done, 1)

            def scores(h, q):
                r, e, i = h % 2, TT * h + q, TILE_OF[q]
                if q == 0:
                    if h == 0:
                        pe.wait_ge(vl_ready, TT)
                        pe.wait_ge(group_rms_ready, 1)
                    pe.wait_ge(pl_ready, 3 * h + 3)
                    pe.wait_ge(krl_ready, 1)
                if e >= 2:
                    pe.wait_ge(exp_ready, e - 1)
                n = P * (i + 1)
                qs = slice(P * i, n)
                bank = pb[3 + q % 2]
                three(bank[:, 0:n], [(qnh[:, r, qs], qnl[:, r, qs], knh[:, r, 0:n], knl[:, r, 0:n]),
                                     (qrh[:, r, qs], qrl[:, r, qs], krh[:, 0:n], krl[:, 0:n])], True, False)
                pe.matmul(bank[:, P * i:n], exact[0:SQUARE, 1, :], exact[0:SQUARE, 2, :],
                          start=False, stop=True).then_inc(s_done, 1)

            def bank_left(h, q):
                before = 5 * h + q - 2
                if before >= 0:
                    bh, bq = divmod(before, 5)
                    if bq == TT:
                        pe.wait_ge(o_copied, bh + 1)
                    else:
                        pe.wait_ge(ptl_ready, TT * bh + bq + 1)

            def turn(h, q):
                i = TILE_OF[q]
                bank_left(h, q)
                pe.wait_ge(p_ready, TT * h + q + 1)
                for kb in range(i + 1):
                    at_ = P_OFF[i] + P * kb
                    last = pe.transpose(turn_bank(h, q)[:, P * kb:P * (kb + 1)], probs[:, h % 2, at_:at_ + P], ident)
                last.then_inc(t_done, 1)

            def head_product(h):
                bank_left(h, TT)
                pe.wait_ge(ptl_ready, TT * h + TT)
                vs = slice(V_HEAD * h, V_HEAD * (h + 1))
                for kb in range(TT):
                    last = three(turn_bank(h, TT)[:, P * kb:SEQ], [(vh[:, kb, vs], vl[:, kb, vs], pth[:, kb, P * kb:SEQ],
                                                                   ptl[:, kb, P * kb:SEQ])], kb == 0, kb == TT - 1)
                last.then_inc(pv_done, 1)

            def scores_and_turns(h, behind=None):
                for q in range(TT):
                    scores(h + 1, q)
                    turn(h, q)
                    if behind is not None and q in behind:
                        behind[q]()

            def head_sum(h):
                pe.wait_ge(gsq_ready, h + 1)
                norm_sum(N_HEAD + h, gsq, AP_BASE[N_HEAD] + h)

            def out_begin(o):
                unit(U_O + o)
                if o == 0:
                    pe.wait_ge(pl_ready, 3 * HEADS)
                if o == 1:
                    pe.wait_ge(exp_ready, HEADS * TT)
                if o == 2:
                    pe.wait_ge(ptl_ready, HEADS * TT)
                if o == 6:
                    pe.wait_ge(x_upd, DT + 2)

            def out_unit(o):
                out_begin(o)
                out_steps(o, range(4)).then_inc(unit_done, 1)

            def out_steps(o, ks):
                upper, pair = O_UNITS[o]
                b = o % 2
                for k in ks:
                    y = 4 * upper + k
                    pe.wait_ge(hl_ready, AP_CONV + y + 1)
                    for d in range(2):
                        w = slice((2 * k + d) * P, (2 * k + d + 1) * P)
                        last = three(pb[O_BANK[2 * pair + d]][:, :], [(wh[b][:, w], wl[b][:, w], hh[:, y, :], hl[:, y, :])],
                                     y == 0, y == DT - 1)
                return last

            conv_sum(0)
            conv_sum(1)
            v_unit(0)
            v_unit(1)
            warm(WARM_HEADS)
            head_part(0, 0)
            conv_sum(2)
            head_part(0, 1)
            conv_sum(3)
            head_part(0, 2)
            head_unit(1)
            scores(0, 0)
            for q in range(1, TT):
                scores(0, q)
                head_part(2, q - 1)
            scores_and_turns(0)
            head_product(0)
            head_unit(3)
            scores_and_turns(1, {0: lambda: conv_spread(0), 2: lambda: conv_spread(1), 3: lambda: conv_spread(2)})
            head_product(1)
            conv_spread(3)
            head_sum(0)
            scores_and_turns(2)
            norm_spread(N_HEAD)
            head_product(2)
            out_unit(0)
            head_sum(1)
            turn(3, 0)
            turn(3, 1)
            out_begin(1)
            out_steps(1, (0, 1))
            turn(3, 2)
            turn(3, 3)
            out_steps(1, (2, 3)).then_inc(unit_done, 1)
            head_product(3)
            norm_spread(N_HEAD + 1)
            out_begin(2)
            out_steps(2, (0, 1))
            head_sum(2)
            out_steps(2, (2, 3)).then_inc(unit_done, 1)
            norm_spread(N_HEAD + 2)
            unit(U_O + 3)
            out_steps(3, (0, 1))
            head_sum(3)
            unit(U_O + 4)
            out_steps(4, (0, 1))
            norm_spread(N_HEAD + 3)
            out_steps(3, (2,))
            out_steps(4, (2,))
            out_steps(3, (3,)).then_inc(unit_done, 1)
            out_steps(4, (3,)).then_inc(unit_done, 1)
            for o in range(5, len(O_UNITS)):
                out_unit(o)
            warm(WARM_SQUARES)
            pe.wait_ge(sq_added, SQ_BASE[N_FFN2] + DT)
            norm_sum(N_FFN2, sacc, AP_BASE[N_FFN2])
            warm(WARM_ROOT)
            norm_spread(N_FFN2)
            warm(WARM_NORMED)

            pe.wait_ge(x_upd, 2 * DT)
            first_pair(U_A2, AP_BASE[N_FFN2])
            with pe.Fori(1, FT) as i:
                up_tile(U_A2, 1, i, N_FFN2)
            down(U_B2, 1, N_FINAL)
            def turn_back(g, ks):
                half, t = divmod(g, TT)
                for k in ks:
                    pe.wait_ge(xg_ready, HALF * half + k + 1)
                    last = pe.transpose(pb[OUT_BANK[g]][:, k * P:(k + 1) * P], xg[:, HALF * half + k, t * P:(t + 1) * P], ident)
                return last

            for g in range(TT):
                turn_back(g, range(HALF)).then_inc(xg_turned, 1)
            turn_back(4, range(HALF - 1))
            turn_back(5, range(HALF - 1))
            pe.wait_ge(sq_added, SQ_BASE[N_FINAL] + DT)
            norm_sum(N_FINAL, sacc, AP_BASE[N_FINAL])
            turn_back(4, (HALF - 1,)).then_inc(xg_turned, 1)
            turn_back(5, (HALF - 1,)).then_inc(xg_turned, 1)
            turn_back(6, range(HALF)).then_inc(xg_turned, 1)
            pe.wait_ge(o_scaled[0], 1)
            turn_back(7, range(HALF)).then_inc(xg_turned, 1)

        @block.vector
        def _(dve):
            def split_lo(n, par):
                dve.wait_ge(hi_ready, n + 1)
                dve.tensor_tensor(wl[par][:, :], raw[par][:, :], wh[par][:, :].bitcast(F32), ALU.subtract).then_inc(lo_ready, 1)

            def clear_sum(n, previous):
                dve.wait_ge(col_done, previous + 1)
                dve.memset(sacc[:, :], 0.0).then_inc(sacc_clear, 1)

            def add_square(n, idx, slot):
                dve.wait_ge(sq_ready, idx + 1)
                dve.wait_ge(sacc_clear, SQ_TURN[n] + 1)
                dve.wait_ge(sq_added, idx)
                dve.tensor_tensor(sacc[:, :], sacc[:, :], sq[:, slot, :], ALU.add).then_inc(sq_added, 1)

            def inverse(n, spread=True):
                dve.wait_ge(rms_ready, n + 1)
                dve.reciprocal(rrms[:, :], rms[:, :]).then_inc(rrms_ready, 1)
                dve.wait_ge(rrms_ready, n + 1)
                if not spread:
                    return
                dve.tensor_copy(rrms_h[:, :], rrms[:, :]).then_inc(rrms_split, 1)
                dve.wait_ge(rrms_split, 2 * n + 1)
                dve.tensor_tensor(rrms_l[:, :], rrms[:, :], rrms_h[:, :].bitcast(F32), ALU.subtract).then_inc(rrms_split, 1)
                if n >= 1:
                    dve.wait_ge(bc_done, SPREAD[n])
                idb = ident.unsqueeze(1).to_broadcast([P, TT, P])
                for part, r in enumerate((rrms_h[:, :].bitcast(F32), rrms_l[:, :])):
                    dve.wait_ge(rrms_split, 2 * n + part + 1)
                    dve.tensor_tensor(diag[:, part, :, :], idb, r.unsqueeze(2).to_broadcast([P, TT, P]),
                                      ALU.mult).then_inc(diag_ready, 1)

            def apply(n, base, tiles, middle=None):
                def lo(j):
                    src, gain, shift, hi_t, lo_t = tiles[j]
                    idx = base + j
                    dve.wait_ge(hh_ready, idx + 1)
                    u = ubuf[:, idx % 3, :]
                    if shift is None:
                        dve.tensor_tensor(lo_t, u, hi_t.bitcast(F32), ALU.subtract).then_inc(hl_ready, 1)
                    else:
                        dve.scalar_tensor_tensor(out=lo_t, in0=u, scalar=shift, in1=hi_t.bitcast(F32),
                                                 op0=ALU.add, op1=ALU.subtract).then_inc(hl_ready, 1)
                dve.wait_ge(bc_done, n + 1)
                for j, (src, gain, shift, hi_t, lo_t) in enumerate(tiles):
                    idx = base + j
                    if idx >= 3:
                        dve.wait_ge(hl_ready, idx - 2)
                    dve.scalar_tensor_tensor(out=ubuf[:, idx % 3, :], in0=src, scalar=gain, in1=norm_bank[:, :],
                                             op0=ALU.mult, op1=ALU.mult).then_inc(u_ready, 1)
                    if middle is None:
                        if j >= 1:
                            lo(j - 1)
                        continue
                    if j == 2:
                        middle()
                    if j >= 2:
                        lo(j - 2)
                if middle is not None:
                    lo(len(tiles) - 2)
                lo(len(tiles) - 1)

            def apply_model(n, which, shift_mod, middle=None):
                apply(SPREAD[n], AP_BASE[n], [(xres[:, k, :], a_cols[:, which, k:k + 1],
                                       mods[:, shift_mod * DT + k:shift_mod * DT + k + 1], hh[:, k, :], hl[:, k, :])
                                      for k in range(DT)], middle)

            def ada(v, k, src, landed_sem, landed_value, steps, first=0):
                dve.wait_ge(landed_sem, landed_value)
                dve.wait_ge(ada_step, steps)
                if k == first:
                    dve.wait_ge(ada_turned, v)
                    dve.tensor_scalar(acc[:, :], src, silu_c[:, k:k + 1], None, ALU.mult).then_inc(ada_step, 1)
                else:
                    dve.scalar_tensor_tensor(out=acc[:, :], in0=src, scalar=silu_c[:, k:k + 1], in1=acc[:, :],
                                             op0=ALU.mult, op1=ALU.add).then_inc(ada_step, 1)

            def fold(v, steps):
                dve.wait_ge(ada_step, steps)
                dve.wait_ge(ada_folded, v)
                if not isinstance(v, int) or v > 0:
                    dve.wait_ge(bc_done, 1)
                dve.transpose(turned[:, :], acc[:, :]).then_inc(ada_turned, 1)
                dve.wait_ge(ada_turned, v + 1)
                dve.wait_ge(ada_summed, v)
                dve.tensor_reduce(folded[:, :], turned.rearrange("p (b c) -> p b c", c=SQUARE), AX_X,
                                  ALU.add).then_inc(ada_folded, 1)

            def mod_bias(v, col):
                bias = vcol
                if isinstance(v, int):
                    dve.wait_ge(ada_direct, v + 1)
                    dve.tensor_tensor(mods[:, col:col + DT], pb[5 + v][:, 0:DT], vcol[:, col:col + DT], ALU.add).then_inc(mods_part, 1)
                    dve.wait_ge(mods_part, v + 1)
                    bias = mods
                dve.wait_ge(ada_summed, v + 1)
                for g in range(QUARTERS):
                    rows = slice(SQUARE * g, SQUARE * (g + 1))
                    sums = pb[4][rows, 0:D_MODEL // SQUARE].rearrange("p (k g) -> p k g", g=QUARTERS)[:, :, g]
                    last = dve.tensor_tensor(mods[rows, bass.ds(col, DT)], sums, bias[rows, bass.ds(col, DT)], ALU.add)
                last.then_inc(mods_ready, 1)

            def up_tile(base, f, i, early=None, middle=None):
                split_lo(base + 2 * i + 2, 0)
                if early is not None:
                    early()
                dve.wait_ge(sig_ready, f * FT + i + 1)
                dve.wait_ge(g_ready, FREE + f * FT + i)
                dve.tensor_tensor(sbuf[:, :], sigb[:, :], pb[0][:, :], ALU.mult).then_inc(s_ready, 1)
                if middle is not None:
                    middle()
                dve.wait_ge(unit_done, base + 2 * i + 2)
                dve.wait_ge(s_ready, FREE + f * FT + i + 1)
                dve.wait_ge(gl_ready, FREE + f * FT + i)
                dve.tensor_tensor(gbuf[:, :], sbuf[:, :], pb[1][:, :], ALU.mult).then_inc(g_ready, 1)
                split_lo(base + 2 * i + 3, 1)
                dve.wait_ge(gh_ready, f * FT + i + 1)
                dve.tensor_tensor(gl[:, bass.ds(i, 1), :], gbuf[:, :].unsqueeze(1), gh[:, bass.ds(i, 1), :].bitcast(F32),
                                  ALU.subtract).then_inc(gl_ready, 1)

            def update(d, bank, gate, done, upd):
                dve.wait_ge(unit_done, done)
                xd = xres[:, bass.ds(d, 1), :]
                dve.scalar_tensor_tensor(out=xd, in0=pb[bank][:, :].unsqueeze(1), scalar=gate, in1=xd,
                                         op0=ALU.mult, op1=ALU.add).then_inc(x_upd, 1)

            def down_pair(base, f, n, upd, m, splits=6):
                for s in range(6):
                    p, kk = divmod(s, 3)
                    if kk == 2:
                        d = 2 * m + p
                        update(d, 2 + p, half_gates[:, f, bass.ds(d, 1)], base + 6 * m + s + 1, upd)
                        add_square(n, SQ_BASE[n] + 2 * m + p, (SQ_BASE[n] + p) % 2)
                    if s < splits:
                        split_lo(base + 6 * m + s + 2, s % 2)

            dve.memset(kst[:, K_COLS:K_COLS + 1], EPS).then_inc(vec_ready, 1)
            dve.memset(sacc[:, :], 0.0).then_inc(sacc_clear, 1)
            for j, free in enumerate((s_ready, g_ready, gl_ready, u_conv, conv_step, yc_ready)):
                dve.memset(vcol[:, V_COLS + j:V_COLS + j + 1], 0.0).then_inc(free, 1)
            step = [0]

            def cs_next(ins):
                step[0] += 1
                ins.then_inc(cs_step, 1)
                dve.wait_ge(cs_step, step[0])

            freq, offset, phase = (kst[:, K_ROPE + i:K_ROPE + i + 1] for i in range(3))
            dve.wait_ge(pos_landed, 16)
            cs_next(dve.tensor_copy(posf[:, :], pos[:, :]))
            cs_next(dve.tensor_scalar(ang[:, :], posf[:, :], freq, None, ALU.mult))
            cs_next(dve.tensor_scalar(turns[:, :], ang[:, :], 1.0 / TURN, offset, ALU.mult, ALU.add))
            cs_next(dve.tensor_scalar(turns[:, :], turns[:, :], ROUND, None, ALU.add))
            cs_next(dve.tensor_scalar(turns[:, :], turns[:, :], ROUND, None, ALU.subtract))
            for part in (TURN1, TURN2):
                cs_next(dve.scalar_tensor_tensor(out=ang[:, :], in0=turns[:, :], scalar=-part, in1=ang[:, :],
                                                 op0=ALU.mult, op1=ALU.add))
            cs_next(dve.scalar_tensor_tensor(out=ang[:, :], in0=turns[:, :], scalar=-TURN3, in1=ang[:, :],
                                             op0=ALU.mult, op1=ALU.add))
            cs_next(dve.tensor_scalar(posf[:, :], ang[:, :], phase, SIN_MAX, ALU.add, ALU.min))
            dve.tensor_scalar(ang[:, :], posf[:, :], -SIN_MAX, None, ALU.max).then_inc(cs_step, 1)
            dve.wait_ge(vec_turned, 2)
            dve.tensor_copy(vcol[:, 0:V_ROWS1], pb[4][:, 0:V_ROWS1]).then_inc(vec_ready, 1)
            dve.tensor_copy(vcol[:, V_ROWS1:V_COLS], pb[5][:, 0:V_COLS - V_ROWS1]).then_inc(vec_ready, 1)
            dve.wait_ge(vec_ready, 3)
            dve.wait_ge(sigc_ready, 1)
            dve.tensor_tensor(silu_c[:, :], sig_c[:, :], vcol[:, V_C:V_C + DT], ALU.mult).then_inc(siluc_ready, 1)
            dve.wait_ge(siluc_ready, 1)
            for k in range(ADA_PE[0], DT):
                ada(0, k, ada_start[:, k, :], start_landed[k // 2], 16, k - ADA_PE[0], ADA_PE[0])
            fold(0, DT - ADA_PE[0])
            inverse(N_FFN1)
            mod_bias(0, DT)
            dve.wait_ge(mods_ready, 1)
            dve.scalar_tensor_tensor(out=a_cols[:, 0, :], in0=mods[:, DT:2 * DT], scalar=1.0, in1=vcol[:, V_G1:V_G1 + DT],
                                     op0=ALU.add, op1=ALU.mult).then_inc(cols_ready, 1)
            dve.wait_ge(cols_ready, 1)

            def shift_vector():
                for k in range(ADA_PE[1], DT):
                    ada(1, k, ada_start[:, DT + k, :], start_landed[4 + k // 2], 16, ADA_START - DT + k, ADA_PE[1])
                fold(1, ADA_START)
                mod_bias(1, 0)
                dve.wait_ge(mods_ready, 2)

            apply_model(N_FFN1, 0, 0, shift_vector)

            up_tile(U_A1, 0, 0)
            with dve.Fori(0, (FT - 1) // 3) as j:
                def ada_steps(ks):
                    for k in ks:
                        ada(j + 2, k, ada_ring[:, k % 4, :], ada_landed[k % 4], 32 * j + 16 * (k // 4 + 1),
                            DT * j + (ADA_START + k))
                up_tile(U_A1, 0, 3 * j + 1, middle=lambda: ada_steps((0, 1, 2)))
                ada_steps((3,))
                up_tile(U_A1, 0, 3 * j + 2, middle=lambda: ada_steps((4, 5, 6)))
                ada_steps((7,))
                up_tile(U_A1, 0, 3 * j + 3, early=lambda: fold(j + 2, DT * j + (ADA_START + DT)))
                mod_bias(j + 2, j * DT + 2 * DT)
            dve.wait_ge(mods_ready, N_MOD)
            for which, mod, gain in ((1, 4, V_GMIX), (2, 7, V_G2)):
                dve.scalar_tensor_tensor(out=a_cols[:, which, :], in0=mods[:, mod * DT:(mod + 1) * DT], scalar=1.0,
                                         in1=vcol[:, gain:gain + DT], op0=ALU.add, op1=ALU.mult).then_inc(cols_ready, 1)
            for f, mod in ((0, 2), (1, 8)):
                dve.tensor_scalar(half_gates[:, f, :], mods[:, mod * DT:(mod + 1) * DT], 0.5, None, ALU.mult).then_inc(cols_ready, 1)
            dve.wait_ge(cols_ready, 5)
            clear_sum(N_MIX, N_FFN1)
            with dve.Fori(0, DT // 2) as m:
                down_pair(U_B1, 0, N_MIX, 0, m)
            inverse(N_MIX)
            apply_model(N_MIX, 1, 3)

            for j in range(KT + QT + 1):
                n = U_Z + j + 2
                if j == 0:
                    clear_sum(N_KV, N_MIX)
                if j == KT + 1:
                    apply(SPREAD[N_KV], AP_BASE[N_KV], [(zkv[:, t, :], vcol[:, V_KVG + t:V_KVG + t + 1], None, ckh[:, t, :], ckl[:, t, :])
                                                for t in range(KT)])
                if j + 2 == KT + QT:
                    dve.wait_ge(hi_ready, n + 1)
                    src = raw[1][:, 0:DT * QK_ROPE].rearrange("p (k f) -> p k f", k=DT)
                    hi = wh[1].rearrange("p (k f) -> p k f", k=DT).bitcast(F32)
                    lo = wl[1].rearrange("p (k f) -> p k f", k=DT)
                    dve.tensor_tensor(lo[:, :, 0:64], src, hi[:, :, 0:64], ALU.subtract)
                    dve.tensor_tensor(lo[:, :, 64:96], src[:, :, 32:64], hi[:, :, 64:96], ALU.subtract)
                    dve.tensor_tensor(lo[:, :, 96:128], src[:, :, 0:32], hi[:, :, 96:128], ALU.subtract).then_inc(lo_ready, 1)
                else:
                    split_lo(n, n % 2)
                if j < KT:
                    add_square(N_KV, SQ_BASE[N_KV] + j, (SQ_BASE[N_KV] + j) % 2)
                elif j < KT + QT:
                    q = j - KT
                    if q == 0:
                        inverse(N_KV)
                        clear_sum(N_Q, N_KV)
                    add_square(N_Q, SQ_BASE[N_Q] + q, (SQ_BASE[N_Q] + q) % 2)
            dve.wait_ge(unit_done, U_CONV)
            dve.wait_ge(cs_ready, 1)
            dve.tensor_tensor(rope[:, :], pb[5][:, :], cs[:, :], ALU.mult).then_inc(kr_roped, 1)
            inverse(N_Q)

            with dve.Fori(0, CT // 2) as m:
                for s in range(6):
                    p, which = divmod(s, 3)
                    i = 2 * m + p
                    banks = CONV_BANKS[p]
                    if which == 1:
                        dve.wait_ge(c_copied, i + 1)
                        dve.wait_ge(unit_done, U_CONV + 6 * m + s + 1)
                        dve.wait_ge(conv_step, FREE + 3 * i)
                        dve.tensor_tensor(ubufc[:, :], cbuf[:, :], pb[banks[1]][:, :], ALU.mult).then_inc(u_conv, 1)
                    if which == 2:
                        def tap(k):
                            return vcol[:, bass.ds(i + (V_CONV + CT * k), 1)]
                        dve.wait_ge(u_conv, FREE + i + 1)
                        dve.wait_ge(yc_ready, FREE + i)
                        dve.tensor_scalar(cacc[:, :], ubufc[:, :], tap(2), None, ALU.mult).then_inc(conv_step, 1)
                        for back in (1, 2):
                            dve.wait_ge(conv_step, FREE + 3 * i + back)
                            dve.scalar_tensor_tensor(out=cacc[:, back:SEQ], in0=ubufc[:, 0:SEQ - back], scalar=tap(2 - back),
                                                     in1=cacc[:, back:SEQ], op0=ALU.mult, op1=ALU.add).then_inc(conv_step, 1)
                        dve.wait_ge(conv_step, FREE + 3 * i + 3)
                        dve.wait_ge(unit_done, U_CONV + 6 * m + s + 1)
                        dve.tensor_tensor(yc[:, bass.ds(i, 1), :], cacc[:, :].unsqueeze(1), pb[banks[2]][:, :].unsqueeze(1),
                                          ALU.mult).then_inc(yc_ready, 1)
                    split_lo(U_CONV + 6 * m + s + 2, s % 2)
            apply(SPREAD[N_Q], AP_BASE[N_Q], [(zq[:, t, :], vcol[:, V_QG + t:V_QG + t + 1], None, cqh[:, t, :], cql[:, t, :])
                                      for t in range(QT)])

            def head_lo(h):
                b = h % 2
                dve.wait_ge(hi_ready, U_H + h + 1)
                src = raw[b][:, 0:QT * QH].rearrange("p (k f) -> p k f", k=QT)
                whf = wh[b][:, :].bitcast(F32)

                def part(t, lo_, hi_):
                    return t[:, lo_:hi_].rearrange("p (k f) -> p k f", k=QT)
                hi_n, hi_r = part(whf, 0, QT * P), part(whf, QT * P, 2 * QT * P)
                lo_n, lo_r = part(wl[b], 0, QT * P), part(wl[b], QT * P, 2 * QT * P)
                dve.tensor_tensor(lo_n, src[:, :, 0:128], hi_n, ALU.subtract)
                dve.tensor_tensor(lo_r[:, :, 0:64], src[:, :, 128:192], hi_r[:, :, 0:64], ALU.subtract)
                dve.tensor_tensor(lo_r[:, :, 64:96], src[:, :, 160:192], hi_r[:, :, 64:96], ALU.subtract)
                dve.tensor_tensor(lo_r[:, :, 96:128], src[:, :, 128:160], hi_r[:, :, 96:128], ALU.subtract)
                dve.tensor_tensor(wl[b][:, 768:1024], raw[b][:, QT * QH:QT * QH + 256], whf[:, 768:1024],
                                  ALU.subtract).then_inc(lo_ready, 1)

            def head_parts_lo(h, between=()):
                r = h % 2
                between = list(between)
                dve.wait_ge(ph_ready, 3 * h + 1)
                dve.tensor_tensor(qnl[:, r, :], pb[0][:, :], qnh[:, r, :].bitcast(F32), ALU.subtract).then_inc(pl_ready, 1)
                if between:
                    between.pop(0)()
                dve.wait_ge(q_done, 2 * h + 2)
                if h == 0:
                    dve.wait_ge(kr_dup, 1)
                else:
                    dve.wait_ge(pl_ready, 3 * h - 1)
                dve.tensor_tensor(rope[:, :], pb[1][:, :], cs[:, :], ALU.mult).then_inc(q_roped, 1)
                if between:
                    between.pop(0)()
                dve.wait_ge(ph_ready, 3 * h + 2)
                dve.wait_ge(q_roped, h + 1)
                dve.tensor_tensor(qrl[:, r, :], rope[:, :], qrh[:, r, :].bitcast(F32), ALU.subtract).then_inc(pl_ready, 1)
                dve.wait_ge(ph_ready, 3 * h + 3)
                dve.tensor_tensor(knl[:, r, :], pb[2][:, :], knh[:, r, :].bitcast(F32), ALU.subtract).then_inc(pl_ready, 1)

            def gained(y, src):
                return [(src, vcol[:, V_OUTG + y:V_OUTG + y + 1], None, hh[:, y, :], hl[:, y, :])]

            def apply_conv(j):
                idx = AP_CONV + j
                dve.wait_ge(bc_done, SPREAD_CONV + j + 1)
                dve.wait_ge(hl_ready, idx - 2)
                dve.scalar_tensor_tensor(out=ubuf[:, idx % 3, :], in0=yc[:, j, :], scalar=vcol[:, V_OUTG + j:V_OUTG + j + 1],
                                         in1=norm_bank[:, :], op0=ALU.mult, op1=ALU.mult).then_inc(u_ready, 1)

            def apply_head(h):
                dve.wait_ge(hl_ready, AP_BASE[N_HEAD] + h)
                apply(SPREAD[N_HEAD + h], AP_BASE[N_HEAD] + h, gained(CT + h, o_raw[:, h, :]))

            def conv_inverse(quarter):
                dve.wait_ge(group_rms_ready, 1)
                part = slice(quarter * P, (quarter + 1) * P)
                dve.reciprocal(sq[:, 1, part], sq[:, 0, part]).then_inc(group_step, 1)

            def conv_split():
                dve.wait_ge(group_step, TT)
                dve.tensor_copy(group_rh[:, :], sq[:, 1, :]).then_inc(group_step, 1)
                dve.wait_ge(group_step, TT + 1)
                dve.tensor_tensor(group_rl[:, :], sq[:, 1, :], group_rh[:, :].bitcast(F32), ALU.subtract).then_inc(group_r_ready, 1)

            def maximum(h, q):
                e, i = TT * h + q, TILE_OF[q]
                dve.wait_ge(s_done, e + 1)
                dve.tensor_reduce(nmax[:, e:e + 1], pb[3 + q % 2][:, 0:P * (i + 1)], AX_X, ALU.max,
                                  negate=True).then_inc(max_ready, 1)
                dve.wait_ge(max_ready, e + 1)
                dve.tensor_scalar(nmax_s[:, e:e + 1], nmax[:, e:e + 1], SCALE, None, ALU.mult).then_inc(nmax_ready, 1)

            def divide(h):
                sums = slice(TT * h, TT * (h + 1))
                dve.wait_ge(exp_ready, TT * (h + 1))
                dve.reciprocal(rinv[:, sums], rsum[:, sums]).then_inc(rinv_ready, 1)
                dve.wait_ge(rinv_ready, h + 1)
                for q in range(TT):
                    e, i = TT * h + q, TILE_OF[q]
                    pr = probs[:, h % 2, P_OFF[i]:P_OFF[i + 1]]
                    dve.tensor_scalar(pr, pr, rinv[:, e:e + 1], None, ALU.mult).then_inc(p_ready, 1)

            def turned_lo(h, q):
                i = TILE_OF[q]
                dve.wait_ge(pth_ready, TT * h + q + 1)
                dve.tensor_tensor(ptl[:, 0:i + 1, P * i:P * (i + 1)],
                                  turn_bank(h, q)[:, 0:P * (i + 1)].rearrange("p (k q) -> p k q", k=i + 1),
                                  pth[:, 0:i + 1, P * i:P * (i + 1)].bitcast(F32), ALU.subtract).then_inc(ptl_ready, 1)

            def maxima_and_turned(h, behind=None, first=0):
                for q in range(TT):
                    if q >= first:
                        maximum(h + 1, q)
                    turned_lo(h, q)
                    if behind is not None and q in behind:
                        behind[q]()

            def unit_lo(n):
                dve.wait_ge(lo_ready, n)
                split_lo(n, n % 2)

            head_lo(0)
            for t in range(TT):
                dve.wait_ge(vh_ready, t + 1)
                dve.tensor_tensor(vl[:, t, :], pb[t][:, :], vh[:, t, :].bitcast(F32), ALU.subtract).then_inc(vl_ready, 1)
            dve.wait_ge(krh_ready, 1)
            dve.tensor_tensor(krl[:, :], pb[5][:, :], krh[:, :].bitcast(F32), ALU.subtract).then_inc(krl_ready, 1)
            head_lo(1)
            head_parts_lo(0)
            conv_inverse(0)
            head_lo(2)
            head_parts_lo(1, (lambda: conv_inverse(1), lambda: maximum(0, 0)))
            maximum(0, 1)
            conv_inverse(2)
            head_lo(3)
            maximum(0, 2)
            maximum(0, 3)
            divide(0)
            maxima_and_turned(0)
            head_parts_lo(2)
            divide(1)
            conv_inverse(3)
            conv_split()
            head_parts_lo(3, (lambda: None, lambda: maximum(2, 0)))
            maxima_and_turned(1, {0: lambda: apply_conv(0), 2: lambda: apply_conv(1), 3: lambda: apply_conv(2)}, first=1)
            divide(2)
            apply_conv(3)
            inverse(N_HEAD)
            maxima_and_turned(2)
            divide(3)
            apply_head(0)
            for q in range(TT):
                turned_lo(3, q)
            inverse(N_HEAD + 1)
            apply_head(1)
            inverse(N_HEAD + 2)
            apply_head(2)
            inverse(N_HEAD + 3)
            apply_head(3)
            dve.wait_ge(bc_done, SPREAD_CONV + CT)
            clear_sum(N_FFN2, N_Q)
            for o in range(3, len(O_UNITS)):
                upper, pair = O_UNITS[o]
                if o == 3:
                    unit_lo(U_O + o + 2)
                if upper:
                    for d in (2 * pair, 2 * pair + 1):
                        update(d, O_BANK[d], mods[:, 5 * DT + d:5 * DT + d + 1], U_O + o + 1, DT)
                if o != 3 and o != len(O_UNITS) - 1:
                    unit_lo(U_O + o + 2)
                if upper:
                    for d in (2 * pair, 2 * pair + 1):
                        add_square(N_FFN2, SQ_BASE[N_FFN2] + d, (SQ_BASE[N_FFN2] + d) % 2)
                if o == len(O_UNITS) - 1:
                    unit_lo(U_O + o + 2)
            inverse(N_FFN2)
            apply_model(N_FFN2, 2, 6)

            with dve.Fori(0, FT) as i:
                up_tile(U_A2, 1, i)
            clear_sum(N_FINAL, N_FFN2)
            with dve.Fori(0, DT // 2 - 1) as m:
                down_pair(U_B2, 1, N_FINAL, 2 * DT, m)
            down_pair(U_B2, 1, N_FINAL, 2 * DT, DT // 2 - 1, 4)
            inverse(N_FINAL, spread=False)
            for g in range(0, DT, 2):
                half, t = divmod(g, TT)
                dve.wait_ge(xg_turned, g + 1)
                dve.tensor_scalar(o_nat[:, t, half * SEQ:(half + 1) * SEQ], pb[OUT_BANK[g]][:, :], rrms[:, t:t + 1], None,
                                  ALU.mult).then_inc(o_scaled[0], 1)


_INS = ["x", "c", "positions", "ada_w", "ada_b", "norm_ffn1_g", "ffn1_w1", "ffn1_w3", "ffn1_w2", "norm_mix_g",
        "w_in", "conv_w", "q_norm_g", "w_uq", "kv_norm_g", "w_ukv", "out_norm_g", "w_out", "norm_ffn2_g",
        "ffn2_w1", "ffn2_w3", "ffn2_w2", "final_norm_g"]


def _constants():
    import numpy as np
    k = np.zeros((P, K_ALL), np.float32)
    r = np.arange(P)
    k[:, K_IDENT:K_IDENT + P] = np.eye(P)
    k[:, K_DUP:K_DUP + P] = r[:, None] % QK_ROPE == r[None, :] % QK_ROPE
    k[:, K_DUP32:K_DUP32 + P] = r[:, None] % SQUARE == r[None, :] % SQUARE
    k[:, K_HALF] = r < P // 2
    k[:, K_HALF + 1] = r >= P // 2
    k[:, K_ONE] = 1.0
    ones, select, hidden = K_COLS, K_COLS + P, K_COLS + 2 * P
    k[:, ones:ones + P] = 1.0
    k[r % SQUARE == 0, select:select + P // 2] = 1.0
    k[r % SQUARE == 1, select + P // 2:select + P] = 1.0
    k[0, hidden + CHUNK:hidden + P] = -1e30
    inv = np.float32(ROPE_THETA) ** (-np.arange(0, QK_ROPE, 2, dtype=np.float32) / np.float32(QK_ROPE))
    k[:, K_ROPE] = inv[r % (QK_ROPE // 2)]
    k[:, K_ROPE + 1] = np.where(r < 64, 0.25, np.where(r < 96, 0.5, 0.0))
    k[:, K_ROPE + 2] = np.where(r < 64, np.pi / 2, np.where(r < 96, np.pi, 0.0))
    return k


def kernel(**inputs):
    import numpy as _np
    import concourse.bacc as _bacc
    from concourse import mybir as _mybir
    from concourse.bass_utils import run_bass_kernel_spmd as _run

    nc = _bacc.Bacc("TRN2", target_bir_lowering=False, num_devices=1)
    arrays, args = {}, []
    for name in _INS:
        a = _np.ascontiguousarray(inputs[name])
        arrays[f"in_{name}_dram"] = a
        args.append(nc.dram_tensor(f"in_{name}_dram", a.shape, _mybir.dt.from_np(a.dtype), kind="ExternalInput").ap())
    k = _constants()
    arrays["in_consts_dram"] = k
    args.append(nc.dram_tensor("in_consts_dram", k.shape, _mybir.dt.float32, kind="ExternalInput").ap())
    args.append(nc.dram_tensor("out_0_dram", (1, SEQ, D_MODEL), _mybir.dt.float32, kind="ExternalOutput").ap())
    hybrid_block(nc, *args)
    r = _run(nc, [arrays], core_ids=[0])
    return r.results[0]["out_0_dram"]
```
